# Optimizing a Trainium2 kernel written in Bass

```python
import jax
import jax.numpy as jnp
from jax import lax
import numpy as np
import math

D_MODEL = 1024
BATCH = 1
SEQ = 256
DEPTH = 2

CTX_LEN = 256
GRID_W = 64
MIX_WIDTH = D_MODEL
A_WIDTH = MIX_WIDTH // 2
A_GROUPS = 4
A_GROUP_CH = A_WIDTH // A_GROUPS
A_CHUNK = 128
NA_HEADS = 8
NA_HEAD_DIM = (MIX_WIDTH - A_WIDTH) // NA_HEADS
NA_WIDTH = NA_HEADS * NA_HEAD_DIM
NA_WIN_ROWS = 8
NA_WIN_COLS = 16
O_NA_Q = 2 * A_WIDTH
O_NA_K = O_NA_Q + NA_WIDTH
O_NA_V = O_NA_K + NA_WIDTH
AB_IN_WIDTH = O_NA_V + NA_WIDTH
FN_WIDTH = MIX_WIDTH // 2
FN_GROUPS = 4
FN_GROUP_CH = FN_WIDTH // FN_GROUPS
GLA_HEADS = 4
GLA_VAL_WIDTH = MIX_WIDTH - FN_WIDTH
GLA_KEY_WIDTH = GLA_VAL_WIDTH // 2
GLA_DK = GLA_KEY_WIDTH // GLA_HEADS
GLA_DV = GLA_VAL_WIDTH // GLA_HEADS
GLA_LOW_RANK = 16
GLA_GATE_TEMP = 16.0
GLA_CHUNK = 64
O_Q = FN_WIDTH
O_K = O_Q + GLA_KEY_WIDTH
O_V = O_K + GLA_KEY_WIDTH
O_G = O_V + GLA_VAL_WIDTH
O_A = O_G + GLA_VAL_WIDTH
CD_IN_WIDTH = O_A + 2 * GLA_LOW_RANK
FFN_HIDDEN = -(-8 * D_MODEL // (3 * 256)) * 256
ROPE_BASE = 10000.0
RMS_EPS = 1e-6
NEG_INF = -1e30
N_EVEN = (DEPTH + 1) // 2
N_ODD = DEPTH // 2


def rmsnorm(x, w):
    xf = x.astype(jnp.float32)
    y = xf * lax.rsqrt(jnp.mean(xf * xf, axis=-1, keepdims=True) + RMS_EPS)
    return (y * w.astype(jnp.float32)).astype(x.dtype)

def modulate(h, shift, scale):
    return h * (1.0 + scale) + shift

def swiglu(h, w_gate, w_up, w_down):
    return (jax.nn.silu(h @ w_gate) * (h @ w_up)) @ w_down

def _rope_1d(xh, pos):
    half = xh.shape[-1] // 2
    inv_freq = ROPE_BASE ** (-jnp.arange(half, dtype=jnp.float32) / half)
    ang = pos.astype(jnp.float32)[:, None] * inv_freq[None, :]
    cos = jnp.cos(ang)[None, :, None, :].astype(xh.dtype)
    sin = jnp.sin(ang)[None, :, None, :].astype(xh.dtype)
    x1, x2 = xh[..., :half], xh[..., half:]
    return jnp.concatenate([x1 * cos - x2 * sin, x2 * cos + x1 * sin], axis=-1)

def axial_rope(x):
    t = jnp.arange(x.shape[1])
    d2 = x.shape[-1] // 2
    return jnp.concatenate([_rope_1d(x[..., :d2], t // GRID_W), _rope_1d(x[..., d2:], t % GRID_W)], axis=-1)

def chunk_token_mlp(uv, norm_w, sgu_w, sgu_b):
    B, T, _ = uv.shape
    uv = jax.nn.gelu(uv)
    u, v = uv[..., :A_WIDTH], uv[..., A_WIDTH:]
    v = rmsnorm(v, norm_w)
    vg = v.reshape(B, T // A_CHUNK, A_CHUNK, A_GROUPS, A_GROUP_CH)
    gate = jnp.einsum('gpq,bnqgc->bnpgc', sgu_w, vg) + sgu_b.T[None, None, :, :, None]
    return u * gate.reshape(B, T, A_WIDTH)

def _na_heads(t):
    return t.reshape(t.shape[0], t.shape[1], NA_HEADS, NA_HEAD_DIM)

def neighbourhood_attention(q, k, v, k_ctx, v_ctx, rel_bias):
    B, T, H, dh = q.shape
    rows = T // GRID_W
    wr = min(NA_WIN_ROWS, rows)
    scale = dh ** -0.5
    qg = q.reshape(B, rows, GRID_W, H, dh)
    kg = k.reshape(B, rows, GRID_W, H, dh)
    vg = v.reshape(B, rows, GRID_W, H, dh)
    col = jnp.arange(GRID_W)
    col_start = jnp.clip(col - NA_WIN_COLS // 2, 0, GRID_W - NA_WIN_COLS)
    col_mask = (col[None, :] >= col_start[:, None]) & (col[None, :] < col_start[:, None] + NA_WIN_COLS)
    col_idx = jnp.clip(col[None, :] - col[:, None] + NA_WIN_COLS - 1, 0, 2 * NA_WIN_COLS - 2)

    def row_block(r):
        row_start = jnp.clip(r - wr // 2, 0, rows - wr)
        qr = lax.dynamic_index_in_dim(qg, r, axis=1, keepdims=False)
        kb = lax.dynamic_slice_in_dim(kg, row_start, wr, axis=1)
        vb = lax.dynamic_slice_in_dim(vg, row_start, wr, axis=1)
        row_idx = row_start + jnp.arange(wr) - r + NA_WIN_ROWS - 1
        bias = jnp.transpose(rel_bias[:, row_idx][:, :, col_idx], (0, 2, 1, 3))
        s_nb = jnp.einsum('bqhd,bwkhd->bhqwk', qr, kb).astype(jnp.float32) * scale + bias[None].astype(jnp.float32)
        s_nb = jnp.where(col_mask[:, None, :], s_nb, NEG_INF).reshape(B, H, GRID_W, wr * GRID_W)
        s_cx = jnp.einsum('bqhd,bchd->bhqc', qr, k_ctx).astype(jnp.float32) * scale
        p = jax.nn.softmax(jnp.concatenate([s_nb, s_cx], axis=-1), axis=-1).astype(v.dtype)
        p_nb = p[..., :wr * GRID_W].reshape(B, H, GRID_W, wr, GRID_W)
        p_cx = p[..., wr * GRID_W:]
        return jnp.einsum('bhqwk,bwkhd->bqhd', p_nb, vb) + jnp.einsum('bhqc,bchd->bqhd', p_cx, v_ctx)

    out = lax.map(row_block, jnp.arange(rows))
    return jnp.moveaxis(out, 0, 1).reshape(B, T, H * dh)

def context_attention(q, k, v):
    B, T, H, dh = q.shape
    s = jnp.einsum('bqhd,bkhd->bhqk', q, k).astype(jnp.float32) * dh ** -0.5
    p = jax.nn.softmax(s, axis=-1).astype(v.dtype)
    return jnp.einsum('bhqk,bkhd->bqhd', p, v).reshape(B, T, H * dh)

def ab_mixer(h, hc, w_in, w_out, sgu_norm_w, sgu_w, sgu_b, rel_bias, with_ctx_out):
    p = h @ w_in
    a_out = chunk_token_mlp(p[..., :O_NA_Q], sgu_norm_w, sgu_w, sgu_b)
    q_l = _na_heads(p[..., O_NA_Q:O_NA_K])
    k_l = _na_heads(p[..., O_NA_K:O_NA_V])
    v_l = _na_heads(p[..., O_NA_V:])
    if with_ctx_out:
        pc = hc @ w_in
        kv_c = pc[..., O_NA_K:]
    else:
        pc = None
        kv_c = hc @ w_in[:, O_NA_K:]
    k_c = _na_heads(kv_c[..., :NA_WIDTH])
    v_c = _na_heads(kv_c[..., NA_WIDTH:])
    b_out = neighbourhood_attention(q_l, k_l, v_l, k_c, v_c, rel_bias)
    y = jnp.concatenate([a_out, b_out], axis=-1) @ w_out
    if not with_ctx_out:
        return y, None
    a_c = chunk_token_mlp(pc[..., :O_NA_Q], sgu_norm_w, sgu_w, sgu_b)
    b_c = context_attention(_na_heads(pc[..., O_NA_Q:O_NA_K]), k_c, v_c)
    y_c = jnp.concatenate([a_c, b_c], axis=-1) @ w_out
    return y, y_c

def fourier_mix(f):
    B, T, _ = f.shape
    fg = f.reshape(B, T, FN_GROUPS, FN_GROUP_CH).astype(jnp.float32)
    out = jnp.fft.fft2(fg, axes=(1, 3), norm='ortho').real
    return out.reshape(B, T, FN_WIDTH).astype(f.dtype)

def _to_heads(t, n_heads):
    B, T, _ = t.shape
    return jnp.transpose(t.reshape(B, T, n_heads, -1), (0, 2, 1, 3))

def log_decay(a_lr, w, b):
    return jax.nn.log_sigmoid((a_lr @ w + b).astype(jnp.float32)) / GLA_GATE_TEMP

def _gla_chunk_terms(k, v, log_a):
    B, H, T, dk = k.shape
    n = T // GLA_CHUNK
    kc = k.reshape(B, H, n, GLA_CHUNK, dk)
    vc = v.reshape(B, H, n, GLA_CHUNK, -1)
    b = jnp.cumsum(log_a.reshape(B, H, n, GLA_CHUNK, dk), axis=3)
    b_last = b[:, :, :, -1:, :]
    kv = jnp.einsum('bhnld,bhnle->bhnde', kc * jnp.exp(b_last - b), vc)
    return kc, vc, b, kv, jnp.exp(b_last[:, :, :, 0, :])

def _gla_scan(kv, decay, s0):
    def step(s, inp):
        d, kv_n = inp
        return d[..., None] * s + kv_n, s
    s_fin, s_prev = lax.scan(step, s0, (jnp.moveaxis(decay, 2, 0), jnp.moveaxis(kv, 2, 0)))
    return jnp.moveaxis(s_prev, 0, 2), s_fin

def gla_final_state(k, v, log_a, s0):
    _, _, _, kv, decay = _gla_chunk_terms(k, v, log_a)
    _, s_fin = _gla_scan(kv, decay, s0)
    return s_fin

def gla_chunked(q, k, v, log_a, s0):
    B, H, T, dk = q.shape
    kc, vc, b, kv, decay = _gla_chunk_terms(k, v, log_a)
    s_prev, s_fin = _gla_scan(kv, decay, s0)
    qe = q.reshape(B, H, -1, GLA_CHUNK, dk) * jnp.exp(b)
    lower = jnp.tril(jnp.ones((GLA_CHUNK, GLA_CHUNK), jnp.float32))
    att = jnp.einsum('bhnld,bhnmd->bhnlm', qe, kc * jnp.exp(-b)) * lower
    o = jnp.einsum('bhnlm,bhnme->bhnle', att, vc) + jnp.einsum('bhnld,bhnde->bhnle', qe, s_prev)
    return o.reshape(B, H, T, -1), s_fin

def gla_output(o, g, head_norm_w):
    B, H, T, dv = o.shape
    o = rmsnorm(jnp.transpose(o, (0, 2, 1, 3)), head_norm_w)
    return (o * jax.nn.silu(g.reshape(B, T, H, dv).astype(jnp.float32))).reshape(B, T, H * dv).astype(g.dtype)

def _split_cd(p):
    return p[..., :O_Q], p[..., O_Q:O_K], p[..., O_K:O_V], p[..., O_V:O_G], p[..., O_G:O_A], p[..., O_A:]

def cd_mixer(h, hc, w_in, w_out, dec_w_f, dec_b_f, dec_w_b, dec_b_b, head_norm_w, with_ctx_out):
    B, T, _ = h.shape
    f32 = jnp.float32
    flip = lambda t: jnp.flip(t, axis=2)
    f_l, q_l, k_l, v_l, g_l, a_l = _split_cd(h @ w_in)
    q_l = axial_rope(q_l.reshape(B, T, GLA_HEADS, GLA_DK)) * GLA_DK ** -0.5
    k_l = axial_rope(k_l.reshape(B, T, GLA_HEADS, GLA_DK))
    ql = jnp.transpose(q_l, (0, 2, 1, 3)).astype(f32)
    kl = jnp.transpose(k_l, (0, 2, 1, 3)).astype(f32)
    vl = _to_heads(v_l, GLA_HEADS).astype(f32)
    la_lf = _to_heads(log_decay(a_l[..., :GLA_LOW_RANK], dec_w_f, dec_b_f), GLA_HEADS)
    la_lb = _to_heads(log_decay(a_l[..., GLA_LOW_RANK:], dec_w_b, dec_b_b), GLA_HEADS)
    if with_ctx_out:
        f_c, q_c, k_c, v_c, g_c, a_c = _split_cd(hc @ w_in)
    else:
        pc = hc @ jnp.concatenate([w_in[:, O_K:O_G], w_in[:, O_A:]], axis=1)
        k_c = pc[..., :GLA_KEY_WIDTH]
        v_c = pc[..., GLA_KEY_WIDTH:GLA_KEY_WIDTH + GLA_VAL_WIDTH]
        a_c = pc[..., GLA_KEY_WIDTH + GLA_VAL_WIDTH:]
    kc = _to_heads(k_c, GLA_HEADS).astype(f32)
    vc = _to_heads(v_c, GLA_HEADS).astype(f32)
    la_cf = _to_heads(log_decay(a_c[..., :GLA_LOW_RANK], dec_w_f, dec_b_f), GLA_HEADS)
    la_cb = _to_heads(log_decay(a_c[..., GLA_LOW_RANK:], dec_w_b, dec_b_b), GLA_HEADS)
    s0 = jnp.zeros((hc.shape[0], GLA_HEADS, GLA_DK, GLA_DV), f32)
    if with_ctx_out:
        qc = (_to_heads(q_c, GLA_HEADS) * GLA_DK ** -0.5).astype(f32)
        o_cf, s_f = gla_chunked(qc, kc, vc, la_cf, s0)
        o_cb, s_b = gla_chunked(flip(qc), flip(kc), flip(vc), flip(la_cb), s0)
        o_c = o_cf + flip(o_cb)
    else:
        s_f = gla_final_state(kc, vc, la_cf, s0)
        s_b = gla_final_state(flip(kc), flip(vc), flip(la_cb), s0)
    o_lf, _ = gla_chunked(ql, kl, vl, la_lf, s_f)
    o_lb, _ = gla_chunked(flip(ql), flip(kl), flip(vl), flip(la_lb), s_b)
    o_l = o_lf + flip(o_lb)
    y = jnp.concatenate([fourier_mix(f_l), gla_output(o_l, g_l, head_norm_w)], axis=-1) @ w_out
    if not with_ctx_out:
        return y, None
    y_c = jnp.concatenate([fourier_mix(f_c), gla_output(o_c, g_c, head_norm_w)], axis=-1) @ w_out
    return y, y_c

def first_inputs(seed: int = 0) -> dict:
    key = jax.random.key(seed)
    ks = jax.random.split(key, 26)
    D = D_MODEL

    def nrm(k, shape, s):
        return jax.random.normal(k, shape, jnp.float32) * s

    return {
        'x': nrm(ks[0], (BATCH, SEQ, D), 1.0),
        'c': nrm(ks[1], (BATCH, D), 1.0),
        'ctx': nrm(ks[2], (BATCH, CTX_LEN, D), 1.0),
        'c_ctx': nrm(ks[3], (D,), 1.0),
        'ada_w': nrm(ks[4], (DEPTH, D, 6 * D), 0.5 * D ** -0.5),
        'ada_b': nrm(ks[5], (DEPTH, 6 * D), 0.02),
        'norm_mix_w': 1.0 + nrm(ks[6], (DEPTH, D), 0.05),
        'norm_ffn_w': 1.0 + nrm(ks[7], (DEPTH, D), 0.05),
        'ffn_w_gate': nrm(ks[8], (DEPTH, D, FFN_HIDDEN), D ** -0.5),
        'ffn_w_up': nrm(ks[9], (DEPTH, D, FFN_HIDDEN), D ** -0.5),
        'ffn_w_down': nrm(ks[10], (DEPTH, FFN_HIDDEN, D), FFN_HIDDEN ** -0.5),
        'ab_w_in': nrm(ks[11], (N_EVEN, D, AB_IN_WIDTH), D ** -0.5),
        'ab_w_out': nrm(ks[12], (N_EVEN, MIX_WIDTH, D), MIX_WIDTH ** -0.5),
        'ab_sgu_norm_w': 1.0 + nrm(ks[13], (N_EVEN, A_WIDTH), 0.05),
        'ab_sgu_w': nrm(ks[14], (N_EVEN, A_GROUPS, A_CHUNK, A_CHUNK), A_CHUNK ** -0.5),
        'ab_sgu_b': 1.0 + nrm(ks[15], (N_EVEN, A_GROUPS, A_CHUNK), 0.05),
        'ab_rel_bias': nrm(ks[16], (N_EVEN, NA_HEADS, 2 * NA_WIN_ROWS - 1, 2 * NA_WIN_COLS - 1), 0.5),
        'cd_w_in': nrm(ks[17], (N_ODD, D, CD_IN_WIDTH), D ** -0.5),
        'cd_w_out': nrm(ks[18], (N_ODD, MIX_WIDTH, D), MIX_WIDTH ** -0.5),
        'cd_decay_w_fwd': nrm(ks[19], (N_ODD, GLA_LOW_RANK, GLA_KEY_WIDTH), GLA_LOW_RANK ** -0.5),
        'cd_decay_b_fwd': nrm(ks[20], (N_ODD, GLA_KEY_WIDTH), 0.1),
        'cd_decay_w_bwd': nrm(ks[21], (N_ODD, GLA_LOW_RANK, GLA_KEY_WIDTH), GLA_LOW_RANK ** -0.5),
        'cd_decay_b_bwd': nrm(ks[22], (N_ODD, GLA_KEY_WIDTH), 0.1),
        'cd_head_norm_w': 1.0 + nrm(ks[23], (N_ODD, GLA_DV), 0.05),
        'final_norm_w': 1.0 + nrm(ks[24], (D,), 0.05),
    }

def first_block(x, c, ctx, c_ctx, ada_w, ada_b, norm_mix_w, norm_ffn_w, ffn_w_gate, ffn_w_up, ffn_w_down,
              ab_w_in, ab_w_out, ab_sgu_norm_w, ab_sgu_w, ab_sgu_b, ab_rel_bias,
              cd_w_in, cd_w_out, cd_decay_w_fwd, cd_decay_b_fwd, cd_decay_w_bwd, cd_decay_b_bwd, cd_head_norm_w,
              final_norm_w):
    silu_c = jax.nn.silu(c)
    silu_cc = jax.nn.silu(c_ctx)
    for i in range(DEPTH):
        last = i == DEPTH - 1
        j = i // 2
        mod = (silu_c @ ada_w[i] + ada_b[i])[:, None, :]
        mod_c = (silu_cc @ ada_w[i] + ada_b[i])[None, None, :]
        sh_m, sc_m, g_m, sh_f, sc_f, g_f = jnp.split(mod, 6, axis=-1)
        shc_m, scc_m, gc_m, shc_f, scc_f, gc_f = jnp.split(mod_c, 6, axis=-1)
        h = modulate(rmsnorm(x, norm_mix_w[i]), sh_m, sc_m)
        hc = modulate(rmsnorm(ctx, norm_mix_w[i]), shc_m, scc_m)
        if i % 2 == 0:
            y, y_c = ab_mixer(h, hc, ab_w_in[j], ab_w_out[j], ab_sgu_norm_w[j], ab_sgu_w[j], ab_sgu_b[j],
                              ab_rel_bias[j], not last)
        else:
            y, y_c = cd_mixer(h, hc, cd_w_in[j], cd_w_out[j], cd_decay_w_fwd[j], cd_decay_b_fwd[j],
                              cd_decay_w_bwd[j], cd_decay_b_bwd[j], cd_head_norm_w[j], not last)
        x = x + g_m * y
        x = x + g_f * swiglu(modulate(rmsnorm(x, norm_ffn_w[i]), sh_f, sc_f), ffn_w_gate[i], ffn_w_up[i], ffn_w_down[i])
        if not last:
            ctx = ctx + gc_m * y_c
            ctx = ctx + gc_f * swiglu(modulate(rmsnorm(ctx, norm_ffn_w[i]), shc_f, scc_f),
                                      ffn_w_gate[i], ffn_w_up[i], ffn_w_down[i])
    return rmsnorm(x, final_norm_w)


HEAD_DIM = 64
N_SLOTS = D_MODEL // HEAD_DIM
A_HEADS = 8
A_LATENT = 128
IDX_HEADS = 8
IDX_DIM = 64
A_TOPK_MAX = 256
B_HEADS = 8
B_KV_HEADS = 2
B_WINDOW = 128
C_HEADS = 16
C_KV_HEADS = 2
CMP_BLOCK = 32
CMP_STRIDE = 16
CMP_HIDDEN = 128
SLC_BLOCK = 64
SLC_COUNT = 8
C_WINDOW = 512
MEM_LEN = 256
X_HEADS = 4
X_HEAD_DIM = 128
D_FF = 2816
N_EXPERTS = 8
TOP_K = 2
D_FF_EXPERT = 3584
REL_BUCKETS = 32
REL_MAX_DIST = 128
Q_BLOCK = 128
SLC_Q_BLOCK = 32
LN_EPS = 1e-5
NEG_INF_2 = -1e30
FORCE_BONUS = 1e6
ALPHA = (2 * DEPTH) ** 0.25
BETA = (8 * DEPTH) ** -0.25
N_EVEN_2 = (DEPTH + 1) // 2
N_ODD_2 = DEPTH // 2
EVEN_WIDTHS = (A_HEADS * HEAD_DIM, A_LATENT, IDX_HEADS * IDX_DIM, IDX_DIM, IDX_HEADS,
               B_HEADS * HEAD_DIM, B_KV_HEADS * HEAD_DIM, B_KV_HEADS * HEAD_DIM)
EVEN_COLS = sum(EVEN_WIDTHS)
ODD_WIDTHS = (C_HEADS * HEAD_DIM,) + (C_KV_HEADS * HEAD_DIM,) * 6 + (3 * C_HEADS,)
ODD_COLS = sum(ODD_WIDTHS)


def split_cols(a, widths):
    cuts = [int(c) for c in np.cumsum(widths)[:-1]]
    return jnp.split(a, cuts, axis=-1)

def layer_norm(x, g, b):
    xf = x.astype(jnp.float32)
    mu = jnp.mean(xf, -1, keepdims=True)
    var = jnp.mean(jnp.square(xf - mu), -1, keepdims=True)
    return ((xf - mu) * lax.rsqrt(var + LN_EPS)).astype(x.dtype) * g + b

def rms_norm(x, g):
    xf = x.astype(jnp.float32)
    y = xf * lax.rsqrt(jnp.mean(jnp.square(xf), -1, keepdims=True) + LN_EPS)
    return y.astype(x.dtype) * g

def rel_bucket(dist):
    n = jnp.maximum(dist, 0)
    max_exact = REL_BUCKETS // 2
    nf = jnp.maximum(n, 1).astype(jnp.float32)
    log_b = max_exact + (jnp.log(nf / max_exact) / math.log(REL_MAX_DIST / max_exact)
                         * (REL_BUCKETS - max_exact)).astype(jnp.int32)
    return jnp.where(n < max_exact, n, jnp.minimum(log_b, REL_BUCKETS - 1))

def banded_attention(q, k, v, rel_tbl, window, sinks=None):
    B, S, H, D = q.shape
    kvh = k.shape[2]
    g = H // kvh
    pad = -(-window // Q_BLOCK) * Q_BLOCK
    span = pad + Q_BLOCK
    kp = jnp.pad(k, ((0, 0), (pad, 0), (0, 0), (0, 0)))
    vp = jnp.pad(v, ((0, 0), (pad, 0), (0, 0), (0, 0)))
    dist = np.arange(Q_BLOCK)[:, None] + pad - np.arange(span)[None, :]
    band = jnp.asarray((dist >= 0) & (dist < window))
    bias = rel_tbl.astype(jnp.float32)[rel_bucket(jnp.asarray(dist))]
    bias = bias.transpose(2, 0, 1).reshape(kvh, g, Q_BLOCK, span)
    key_off = jnp.arange(span) - pad

    def block(n):
        t0 = n * Q_BLOCK
        qb = lax.dynamic_slice_in_dim(q, t0, Q_BLOCK, 1).reshape(B, Q_BLOCK, kvh, g, D)
        kb = lax.dynamic_slice_in_dim(kp, t0, span, 1)
        vb = lax.dynamic_slice_in_dim(vp, t0, span, 1)
        logits = jnp.einsum('bqkgd,bskd->bkgqs', qb, kb).astype(jnp.float32) * D ** -0.5 + bias
        ok = band & (t0 + key_off >= 0)[None, :]
        logits = jnp.where(ok, logits, NEG_INF_2)
        if sinks is None:
            p = jax.nn.softmax(logits, axis=-1)
        else:
            s = sinks.astype(jnp.float32).reshape(kvh, g, 1, 1)
            m = jnp.maximum(jnp.max(logits, -1, keepdims=True), s)
            e = jnp.exp(logits - m)
            p = e / (jnp.sum(e, -1, keepdims=True) + jnp.exp(s - m))
        o = jnp.einsum('bkgqs,bskd->bqkgd', p.astype(v.dtype), vb)
        return o.reshape(B, Q_BLOCK, H, D)

    out = lax.map(block, jnp.arange(S // Q_BLOCK))
    return jnp.moveaxis(out, 0, 1).reshape(B, S, H, D)

def dsa_attention(q_a, c_kv, q_i, k_i, w_i, ckv_gain, w_uk, w_uv, rel_tbl):
    B, S, _ = q_a.shape
    topk = min(A_TOPK_MAX, S // 4)
    q_lat = jnp.einsum('bshd,hdc->bshc', q_a.reshape(B, S, A_HEADS, HEAD_DIM), w_uk)
    c = rms_norm(c_kv, ckv_gain)
    qi = q_i.reshape(B, S, IDX_HEADS, IDX_DIM)
    wi = w_i * IDX_HEADS ** -0.5
    tbl = rel_tbl.astype(jnp.float32)
    kpos = jnp.arange(S)

    def block(n):
        t0 = n * Q_BLOCK
        qpos = t0 + jnp.arange(Q_BLOCK)
        qi_b = lax.dynamic_slice_in_dim(qi, t0, Q_BLOCK, 1)
        wi_b = lax.dynamic_slice_in_dim(wi, t0, Q_BLOCK, 1)
        ql_b = lax.dynamic_slice_in_dim(q_lat, t0, Q_BLOCK, 1)
        act = jax.nn.relu(jnp.einsum('bqhd,bsd->bqhs', qi_b, k_i) * IDX_DIM ** -0.5)
        score = jnp.einsum('bqh,bqhs->bqs', wi_b, act).astype(jnp.float32)
        score = jnp.where(kpos[None, :] <= qpos[:, None], score, NEG_INF_2)
        _, sel = lax.top_k(score, topk)
        c_sel = jax.vmap(lambda cb, sb: cb[sb])(c, sel)
        dist = qpos[None, :, None] - sel
        bias = tbl[rel_bucket(dist)].transpose(0, 1, 3, 2)
        lg = jnp.einsum('bqhc,bqkc->bqhk', ql_b, c_sel).astype(jnp.float32) * HEAD_DIM ** -0.5 + bias
        lg = jnp.where((dist >= 0)[:, :, None, :], lg, NEG_INF_2)
        p = jax.nn.softmax(lg, axis=-1).astype(c.dtype)
        o_lat = jnp.einsum('bqhk,bqkc->bqhc', p, c_sel)
        return jnp.einsum('bqhc,hcd->bqhd', o_lat, w_uv)

    out = lax.map(block, jnp.arange(S // Q_BLOCK))
    return jnp.moveaxis(out, 0, 1).reshape(B, S, A_HEADS, HEAD_DIM)

def compress_blocks(kv, pe, w1, w2):
    B, S, G, D = kv.shape
    n_cmp = (S - CMP_BLOCK) // CMP_STRIDE + 1
    idx = np.arange(n_cmp)[:, None] * CMP_STRIDE + np.arange(CMP_BLOCK)[None, :]
    blk = kv[:, idx] + pe[None, None, :, None, :]
    blk = blk.transpose(0, 1, 3, 2, 4).reshape(B, n_cmp, G, CMP_BLOCK * D)
    return jax.nn.gelu(blk @ w1) @ w2

def nsa_attention(q, k_cmp, v_cmp, k_slc, v_slc, k_win, v_win, gate_logits,
                  pe_k, w1_k, w2_k, pe_v, w1_v, w2_v, rel_tbl):
    B, S, H, D = q.shape
    G = C_KV_HEADS
    hpg = H // G
    qg = q.reshape(B, S, G, hpg, D)
    scale = D ** -0.5
    tbl = rel_tbl.astype(jnp.float32)
    pos = np.arange(S)

    n_cmp = (S - CMP_BLOCK) // CMP_STRIDE + 1
    kc = compress_blocks(k_cmp, pe_k, w1_k, w2_k)
    vc = compress_blocks(v_cmp, pe_v, w1_v, w2_v)
    cmp_end = np.arange(n_cmp) * CMP_STRIDE + CMP_BLOCK - 1
    dist_c = pos[:, None] - cmp_end[None, :]
    valid_c = jnp.asarray(dist_c >= 0)
    bias_c = tbl[rel_bucket(jnp.asarray(dist_c))].transpose(2, 0, 1).reshape(G, hpg, S, n_cmp)
    lg = jnp.einsum('bsghd,bngd->bghsn', qg, kc).astype(jnp.float32) * scale + bias_c
    p_cmp = jax.nn.softmax(jnp.where(valid_c, lg, NEG_INF_2), axis=-1) * valid_c
    o_cmp = jnp.einsum('bghsn,bngd->bsghd', p_cmp.astype(vc.dtype), vc).reshape(B, S, H, D)

    n_slc = S // SLC_BLOCK
    n_sel = min(SLC_COUNT, n_slc)
    cs = np.arange(n_cmp)[:, None] * CMP_STRIDE
    ss = np.arange(n_slc)[None, :] * SLC_BLOCK
    overlap = jnp.asarray(((cs < ss + SLC_BLOCK) & (cs + CMP_BLOCK > ss)).astype(np.float32))
    p_slc = jnp.einsum('bghsn,nj->bgsj', p_cmp, overlap)
    blk = pos // SLC_BLOCK
    jj = np.arange(n_slc)
    forced = (jj[None, :] == 0) | (jj[None, :] == blk[:, None]) | (jj[None, :] == blk[:, None] - 1)
    admissible = jj[None, :] * SLC_BLOCK <= pos[:, None]
    score = jnp.where(jnp.asarray(admissible),
                      p_slc + FORCE_BONUS * jnp.asarray(forced.astype(np.float32)), NEG_INF_2)
    _, sel = lax.top_k(score, n_sel)

    kb = k_slc.reshape(B, n_slc, SLC_BLOCK, G, D).transpose(0, 3, 1, 2, 4)
    vb = v_slc.reshape(B, n_slc, SLC_BLOCK, G, D).transpose(0, 3, 1, 2, 4)
    bi = jnp.arange(B)[:, None, None, None]
    gi = jnp.arange(G)[None, :, None, None]
    tbl_g = tbl.reshape(REL_BUCKETS, G, hpg).transpose(1, 0, 2)
    in_blk = jnp.arange(SLC_BLOCK)
    n_keys = n_sel * SLC_BLOCK

    def slc_block(n):
        t0 = n * SLC_Q_BLOCK
        qpos = t0 + jnp.arange(SLC_Q_BLOCK)
        qb = lax.dynamic_slice_in_dim(qg, t0, SLC_Q_BLOCK, 1)
        sb = lax.dynamic_slice_in_dim(sel, t0, SLC_Q_BLOCK, 2)
        ks = kb[bi, gi, sb].reshape(B, G, SLC_Q_BLOCK, n_keys, D)
        vs = vb[bi, gi, sb].reshape(B, G, SLC_Q_BLOCK, n_keys, D)
        kpos = (sb[..., None] * SLC_BLOCK + in_blk).reshape(B, G, SLC_Q_BLOCK, n_keys)
        dist = qpos[None, None, :, None] - kpos
        bias = tbl_g[gi, rel_bucket(dist)].transpose(0, 1, 4, 2, 3)
        lg2 = jnp.einsum('bqghd,bgqsd->bghqs', qb, ks).astype(jnp.float32) * scale + bias
        lg2 = jnp.where((dist >= 0)[:, :, None], lg2, NEG_INF_2)
        p = jax.nn.softmax(lg2, axis=-1).astype(vs.dtype)
        o = jnp.einsum('bghqs,bgqsd->bqghd', p, vs)
        return o.reshape(B, SLC_Q_BLOCK, H, D)

    o_slc = lax.map(slc_block, jnp.arange(S // SLC_Q_BLOCK))
    o_slc = jnp.moveaxis(o_slc, 0, 1).reshape(B, S, H, D)

    o_win = banded_attention(q, k_win, v_win, rel_tbl, C_WINDOW)

    gt = jax.nn.sigmoid(gate_logits).reshape(B, S, H, 3)
    return gt[..., 0:1] * o_cmp + gt[..., 1:2] * o_slc + gt[..., 2:3] * o_win

def even_mixer(x, w_in, ckv_gain, w_uk, w_uv, sinks, w_out, rel_table):
    B, S, _ = x.shape
    q_a, c_kv, q_i, k_i, w_i, q_b, k_b, v_b = split_cols(x @ w_in, EVEN_WIDTHS)
    o_a = dsa_attention(q_a, c_kv, q_i, k_i, w_i, ckv_gain, w_uk, w_uv, rel_table[:, :A_HEADS])
    o_b = banded_attention(q_b.reshape(B, S, B_HEADS, HEAD_DIM),
                           k_b.reshape(B, S, B_KV_HEADS, HEAD_DIM),
                           v_b.reshape(B, S, B_KV_HEADS, HEAD_DIM),
                           rel_table[:, A_HEADS:A_HEADS + B_HEADS], B_WINDOW, sinks)
    o = jnp.concatenate([o_a.reshape(B, S, -1), o_b.reshape(B, S, -1)], axis=-1)
    return o @ w_out

def odd_mixer(x, w_in, pe_k, w1_k, w2_k, pe_v, w1_v, w2_v, w_out, rel_table):
    B, S, _ = x.shape
    q, kc, vc, ks, vs, kw, vw, gl = split_cols(x @ w_in, ODD_WIDTHS)
    r = lambda a, h: a.reshape(B, S, h, HEAD_DIM)
    o = nsa_attention(r(q, C_HEADS), r(kc, C_KV_HEADS), r(vc, C_KV_HEADS), r(ks, C_KV_HEADS),
                      r(vs, C_KV_HEADS), r(kw, C_KV_HEADS), r(vw, C_KV_HEADS), gl,
                      pe_k, w1_k, w2_k, pe_v, w1_v, w2_v, rel_table[:, :C_HEADS])
    return o.reshape(B, S, C_HEADS * HEAD_DIM) @ w_out

def cross_attention(x, mem, w_q, w_k, w_v, w_o):
    B, S, _ = x.shape
    M = mem.shape[1]
    q = (x @ w_q).reshape(B, S, X_HEADS, X_HEAD_DIM)
    k = (mem @ w_k).reshape(B, M, X_HEADS, X_HEAD_DIM)
    v = (mem @ w_v).reshape(B, M, X_HEADS, X_HEAD_DIM)
    lg = jnp.einsum('bshd,bmhd->bhsm', q, k).astype(jnp.float32) * X_HEAD_DIM ** -0.5
    p = jax.nn.softmax(lg, axis=-1).astype(v.dtype)
    o = jnp.einsum('bhsm,bmhd->bshd', p, v).reshape(B, S, X_HEADS * X_HEAD_DIM)
    return o @ w_o

def dense_swiglu(x, w_gate, w_up, w_down):
    return (jax.nn.silu(x @ w_gate) * (x @ w_up)) @ w_down

def moe_swiglu(x, w_router, w_gate, w_up, w_down):
    logits = (x @ w_router).astype(jnp.float32)
    top_val, top_idx = lax.top_k(logits, TOP_K)
    top_w = jax.nn.softmax(top_val, axis=-1)
    gate = jnp.einsum('bsk,bske->bse', top_w,
                      jax.nn.one_hot(top_idx, N_EXPERTS, dtype=jnp.float32)).astype(x.dtype)
    y = jnp.zeros_like(x)
    for e in range(N_EXPERTS):
        h = jax.nn.silu(x @ w_gate[e]) * (x @ w_up[e])
        y = y + gate[..., e:e + 1] * (h @ w_down[e])
    return y

def second_inputs(seed: int = 0) -> dict:
    key = jax.random.key(seed)
    ks = iter(jax.random.split(key, 32))

    def nrm(shape, scale):
        return jax.random.normal(next(ks), shape, jnp.float32) * scale

    D = D_MODEL
    XW = X_HEADS * X_HEAD_DIM
    CW = CMP_BLOCK * HEAD_DIM
    return {
        'x': nrm((BATCH, SEQ, D), 1.0),
        'mem': nrm((BATCH, MEM_LEN, D), 1.0),
        'rel_table': nrm((REL_BUCKETS, N_SLOTS), 0.2),
        'ev_w_in': nrm((N_EVEN_2, D, EVEN_COLS), D ** -0.5),
        'ev_ckv_gain': 1.0 + nrm((N_EVEN_2, A_LATENT), 0.02),
        'ev_w_uk': nrm((N_EVEN_2, A_HEADS, HEAD_DIM, A_LATENT), HEAD_DIM ** -0.5),
        'ev_w_uv': nrm((N_EVEN_2, A_HEADS, A_LATENT, HEAD_DIM), A_LATENT ** -0.5),
        'ev_sinks': nrm((N_EVEN_2, B_HEADS), 0.5),
        'ev_w_out': nrm((N_EVEN_2, N_SLOTS * HEAD_DIM, D), BETA * (N_SLOTS * HEAD_DIM) ** -0.5),
        'od_w_in': nrm((N_ODD_2, D, ODD_COLS), D ** -0.5),
        'od_pe_k': nrm((N_ODD_2, CMP_BLOCK, HEAD_DIM), 0.1),
        'od_w1_k': nrm((N_ODD_2, CW, CMP_HIDDEN), CW ** -0.5),
        'od_w2_k': nrm((N_ODD_2, CMP_HIDDEN, HEAD_DIM), CMP_HIDDEN ** -0.5),
        'od_pe_v': nrm((N_ODD_2, CMP_BLOCK, HEAD_DIM), 0.1),
        'od_w1_v': nrm((N_ODD_2, CW, CMP_HIDDEN), CW ** -0.5),
        'od_w2_v': nrm((N_ODD_2, CMP_HIDDEN, HEAD_DIM), CMP_HIDDEN ** -0.5),
        'od_w_out': nrm((N_ODD_2, C_HEADS * HEAD_DIM, D), BETA * (C_HEADS * HEAD_DIM) ** -0.5),
        'xa_w_q': nrm((DEPTH, D, XW), D ** -0.5),
        'xa_w_k': nrm((DEPTH, D, XW), D ** -0.5),
        'xa_w_v': nrm((DEPTH, D, XW), D ** -0.5),
        'xa_w_o': nrm((DEPTH, XW, D), BETA * XW ** -0.5),
        'ff_w_gate': nrm((N_EVEN_2, D, D_FF), D ** -0.5),
        'ff_w_up': nrm((N_EVEN_2, D, D_FF), D ** -0.5),
        'ff_w_down': nrm((N_EVEN_2, D_FF, D), BETA * D_FF ** -0.5),
        'moe_w_router': nrm((N_ODD_2, D, N_EXPERTS), D ** -0.5),
        'moe_w_gate': nrm((N_ODD_2, N_EXPERTS, D, D_FF_EXPERT), D ** -0.5),
        'moe_w_up': nrm((N_ODD_2, N_EXPERTS, D, D_FF_EXPERT), D ** -0.5),
        'moe_w_down': nrm((N_ODD_2, N_EXPERTS, D_FF_EXPERT, D), BETA * D_FF_EXPERT ** -0.5),
        'ln_g': 1.0 + nrm((DEPTH, 3, D), 0.02),
        'ln_b': nrm((DEPTH, 3, D), 0.02),
    }

def second_block(x, mem, rel_table, ev_w_in, ev_ckv_gain, ev_w_uk, ev_w_uv, ev_sinks, ev_w_out,
              od_w_in, od_pe_k, od_w1_k, od_w2_k, od_pe_v, od_w1_v, od_w2_v, od_w_out,
              xa_w_q, xa_w_k, xa_w_v, xa_w_o, ff_w_gate, ff_w_up, ff_w_down,
              moe_w_router, moe_w_gate, moe_w_up, moe_w_down, ln_g, ln_b):
    h = x
    for i in range(DEPTH):
        j = i // 2
        if i % 2 == 0:
            mix = even_mixer(h, ev_w_in[j], ev_ckv_gain[j], ev_w_uk[j], ev_w_uv[j], ev_sinks[j],
                             ev_w_out[j], rel_table)
        else:
            mix = odd_mixer(h, od_w_in[j], od_pe_k[j], od_w1_k[j], od_w2_k[j], od_pe_v[j],
                            od_w1_v[j], od_w2_v[j], od_w_out[j], rel_table)
        h = layer_norm(ALPHA * h + mix, ln_g[i, 0], ln_b[i, 0])
        xa = cross_attention(h, mem, xa_w_q[i], xa_w_k[i], xa_w_v[i], xa_w_o[i])
        h = layer_norm(ALPHA * h + xa, ln_g[i, 1], ln_b[i, 1])
        if i % 2 == 0:
            ff = dense_swiglu(h, ff_w_gate[j], ff_w_up[j], ff_w_down[j])
        else:
            ff = moe_swiglu(h, moe_w_router[j], moe_w_gate[j], moe_w_up[j], moe_w_down[j])
        h = layer_norm(ALPHA * h + ff, ln_g[i, 2], ln_b[i, 2])
    return h


def setup_inputs(seed=0):
    out = dict(first_inputs(seed))
    for name, value in second_inputs(seed + 1).items():
        if name != "x":
            out[name + "_2"] = value
    return out


def reference(
    x, c, ctx, c_ctx, ada_w, ada_b, norm_mix_w, norm_ffn_w, ffn_w_gate, ffn_w_up, ffn_w_down,
    ab_w_in, ab_w_out, ab_sgu_norm_w, ab_sgu_w, ab_sgu_b, ab_rel_bias, cd_w_in, cd_w_out,
    cd_decay_w_fwd, cd_decay_b_fwd, cd_decay_w_bwd, cd_decay_b_bwd, cd_head_norm_w,
    final_norm_w, mem_2, rel_table_2, ev_w_in_2, ev_ckv_gain_2, ev_w_uk_2, ev_w_uv_2,
    ev_sinks_2, ev_w_out_2, od_w_in_2, od_pe_k_2, od_w1_k_2, od_w2_k_2, od_pe_v_2, od_w1_v_2,
    od_w2_v_2, od_w_out_2, xa_w_q_2, xa_w_k_2, xa_w_v_2, xa_w_o_2, ff_w_gate_2, ff_w_up_2,
    ff_w_down_2, moe_w_router_2, moe_w_gate_2, moe_w_up_2, moe_w_down_2, ln_g_2, ln_b_2,
):
    x = first_block(
        x, c, ctx, c_ctx, ada_w, ada_b, norm_mix_w, norm_ffn_w, ffn_w_gate, ffn_w_up,
        ffn_w_down, ab_w_in, ab_w_out, ab_sgu_norm_w, ab_sgu_w, ab_sgu_b, ab_rel_bias, cd_w_in,
        cd_w_out, cd_decay_w_fwd, cd_decay_b_fwd, cd_decay_w_bwd, cd_decay_b_bwd,
        cd_head_norm_w, final_norm_w,
    )
    return second_block(
        x, mem_2, rel_table_2, ev_w_in_2, ev_ckv_gain_2, ev_w_uk_2, ev_w_uv_2, ev_sinks_2,
        ev_w_out_2, od_w_in_2, od_pe_k_2, od_w1_k_2, od_w2_k_2, od_pe_v_2, od_w1_v_2, od_w2_v_2,
        od_w_out_2, xa_w_q_2, xa_w_k_2, xa_w_v_2, xa_w_o_2, ff_w_gate_2, ff_w_up_2, ff_w_down_2,
        moe_w_router_2, moe_w_gate_2, moe_w_up_2, moe_w_down_2, ln_g_2, ln_b_2,
    )


_drawn_inputs = setup_inputs


def setup_inputs(seed=0):
    import zlib

    import numpy as np

    out = dict(_drawn_inputs(seed))
    spreads = {}
    factors = {'ab_sgu_norm_w': 4.17,
     'ab_sgu_b': 4.471,
     'ab_rel_bias': 4.228,
     'cd_decay_b_fwd': 5.575,
     'cd_decay_b_bwd': 6.329,
     'cd_head_norm_w': 4.107,
     'ev_ckv_gain_2': 6.802,
     'ev_sinks_2': 52.553,
     'od_pe_k_2': 37.632,
     'od_pe_v_2': 4.453}
    for name, (base, spread) in spreads.items():
        noise = np.random.default_rng([zlib.crc32(name.encode()), seed]).standard_normal(out[name].shape)
        drawn = base * np.exp(spread * noise) if base else spread * noise
        out[name] = jnp.asarray(drawn.astype(out[name].dtype))
    for name, factor in factors.items():
        out[name] = (out[name] * factor).astype(out[name].dtype)
    return out
```

```python
from contextlib import ExitStack
import math

import numpy as np

import concourse.bass as bass
from concourse import mybir

F32 = mybir.dt.float32
U32 = mybir.dt.uint32
F32R = mybir.dt.float32r
ALU = mybir.AluOpType
ACT = mybir.ActivationFunctionType
AX_X = mybir.AxisListType.X

P = 128
D = 1024
DC = D // P
SEQ = 256
CTX = 256
TT = SEQ + CTX
FFN = 2816
FC = FFN // P
EXPERTS = 8
FE = 3584
NEG = -1e30
RMS_EPS = 1e-6
LN_EPS = 1e-5
ALPHA = 4 ** 0.25

TILES = 16
SLOT = TILES * P
RING = 6
BANKS = 8
FB = 4

SMALL = [
    ("c2", DC * 2), ("ada_b", 192), ("norm_mix_w", 4 * DC), ("norm_ffn_w", 4 * DC), ("sgu_norm_w", 4),
    ("final_norm_w", DC), ("ln_g", 6 * DC), ("ln_b", 6 * DC), ("ckv_gain", 1), ("decay_b", 4), ("head_norm_w", 1),
    ("ident", P), ("ones", P), ("rot", P), ("cos", SEQ), ("sin", SEQ),
    ("dft_ch", 2 * P), ("dft_cos", 2 * SEQ), ("dft_nsin", 2 * SEQ),
    ("w_idx", DC * 8), ("w_router", DC * EXPERTS), ("w_gates", DC * 48), ("w_lowrank", DC * 32),
    ("w_decay", 2 * 256), ("w_uk", 4 * P), ("w_uv", 8 * 64), ("w2_k", 64), ("w2_v", 64), ("pe_k", 32), ("pe_v", 32),
    ("sinks", 8), ("tri", 2 * P), ("chunk_start", TT), ("expert_id", EXPERTS), ("cmp_row_ok", 2), ("eps", 2),
    ("slot_id", P), ("earlier", P),
]
COL, _at = {}, 0
for _name, _w in SMALL:
    COL[_name] = (_at, _w)
    _at += _w
N_SMALL = _at
ARENA = 25472
PASSES = 2
MOE_TURNS = FE // P // FB * (2 * FB + 2) + 4 + 4 + 2
LN_EVENTS = 6 * DC

SLOTS_ADA = 96 * DC // TILES
SLOTS_FFN = FC * 3 * DC // TILES
SLOTS_MOE = EXPERTS * (FE // P) * 3 * DC // TILES
SLOTS_EXPERT = SLOTS_MOE // EXPERTS
FFN_AT = [SLOTS_ADA + 10 + 4]
FFN_AT.append(FFN_AT[0] + SLOTS_FFN + 8 + 4)
FFN_AT.append(FFN_AT[1] + SLOTS_FFN + 8 + 4 + 8)
N_SLOTS = SLOTS_ADA + 10 + 4 + SLOTS_FFN + 8 + 4 + SLOTS_FFN + 8 + 4 + 8 + SLOTS_FFN + 7 + 4 + 4 + 8 + SLOTS_MOE



class Tally:

    def __init__(self):
        self.count, self.per, self.i = {}, {}, None

    def up(self, name, n=1):
        self.count[name] = self.count.get(name, 0) + n
        v = self.count[name]
        return v + self.i * self.per[name] if self.i is not None and name in self.per else v

    def enter(self, i, per):
        self.i, self.per, self.before = i, per, dict(self.count)

    def leave(self, times):
        for name, n in list(self.count.items()):
            step = n - self.before.get(name, 0)
            assert step == self.per.get(name, 0), (name, step, self.per.get(name))
            self.count[name] = n + step * (times - 1)
        self.i = None


def build(nc, stream, small, x_t, ctx_t, mem_t, ab_bias, sgu, t5_bias, band_bias, cmp_bias, out):
    with ExitStack() as ctx:
        def sb(name, cols, dt=F32):
            return ctx.enter_context(nc.sbuf_tensor(name, [P, cols], dt))

        sems = {}

        def sem(name):
            if name not in sems:
                sems[name] = ctx.enter_context(nc.semaphore(name))
            return sems[name]

        with ExitStack() as plain:
            ring, hs, arena = (plain.enter_context(nc.sbuf_tensor(name, [P, cols], F32)) for name, cols in (
                ("ring", RING * SLOT),
                ("h_normed", DC * TT),
                ("arena", ARENA)))
        ring_part, hs_part = sb("ring_part", RING * SLOT, F32R), sb("h_part", DC * TT, F32R)
        arena_part = sb("arena_part", ARENA, F32R)
        xs = sb("x_stream", DC * TT)
        consts = sb("consts", N_SMALL)
        mod = sb("mod", 2 * 48 * 2)
        mod_scale = sb("mod_scale", 2 * 2 * DC * 2)
        silu_c = sb("silu_c", 2 * DC)
        rstd = sb("rstd", TT)
        mean = sb("mean", SEQ)
        stats = sb("stats", 96)
        whole = sb("whole_numbers", 16, U32)
        PS = [ctx.enter_context(nc.psum_tensor(f"bank{i}", [P, 512], F32)) for i in range(BANKS)]

        xv = xs[:, :].rearrange("p (c t) -> p c t", c=DC)
        hv = hs[:, :].rearrange("p (c t) -> p c t", c=DC)
        h_part = hs_part[:, :].rearrange("p (c t) -> p c t", c=DC)
        modv = mod[:, :].rearrange("p (l n s) -> p l n s", l=2, n=48)
        scalev = mod_scale[:, :].rearrange("p (l m c s) -> p l m c s", l=2, m=2, c=DC)

        def small_at(name, pattern=None, **dims):
            a, w = COL[name]
            v = consts[:, a:a + w]
            return v.rearrange(pattern, **dims) if pattern else v

        ident, ones = small_at("ident"), small_at("ones")

        def area(at, cols, pattern=None, **dims):
            assert at + cols <= ARENA, (at, cols)
            v = arena[:, at:at + cols]
            return v.rearrange(pattern, **dims) if pattern else v

        def part_area(at, cols, pattern=None, **dims):
            v = arena_part[:, at:at + cols]
            return v.rearrange(pattern, **dims) if pattern else v

        def shift(l, m, c, s):
            return modv[:, l, 24 * m + c, s:s + 1]

        def gain(l, m, c, s):
            return modv[:, l, 24 * m + 16 + c, s:s + 1]

        T5, BAND, CMPB = ARENA - 6656, ARENA - 2560, ARENA - 512
        t5v = area(T5, 4096, "p (h k) -> p h k", h=16)
        bandv = area(BAND, 2048, "p (h k) -> p h k", h=8)
        cmpv = area(CMPB, 512, "p (q h n) -> p q h n", q=2, h=16)
        AT = T5 - 4120
        score_buf = [area(AT + 516 * i, 516) for i in range(3)]
        exp_buf = [area(AT + 1548 + 516 * i, 516) for i in range(3)]
        pt_buf = [area(AT + 3096 + 512 * i, 512) for i in range(2)]
        sqv = area(0, DC * TT, "p (c t) -> p c t", c=DC)
        ada_rows = area(4096, 24 * P)
        uT = area(0, 2048, "p (g t) -> p g t", g=4)
        v_tok = area(2048, 2048, "p (t c) -> p t c", t=4)
        qT = area(4096, 2048, "p (c t) -> p c t", c=4)
        kT = area(6144, 2048, "p (c t) -> p c t", c=4)
        v_att = area(8192, 2048, "p (t c) -> p t c", t=4)
        gate_tmp = area(10240, 512)
        v_junk = area(10752, 512)
        ab_biasv = area(T5, 4096, "p (h q k) -> p h q k", h=8, q=2)
        sgu_w = area(T5 + 4096, 512, "p (g q) -> p g q", g=4)
        sgu_b = area(T5 + 4608, 512, "p (g q) -> p g q", g=4)
        in_high = part_area(0, 4096, "p (c t) -> p c t", c=DC)
        act_buf = area(17408, 512)
        act_low = part_area(4096, 2048, "p (f t) -> p f t", f=FB)
        act_high = part_area(6144, 2048, "p (f t) -> p f t", f=FB)
        down_acc = area(8192, 4096, "p (c t) -> p c t", c=DC)
        silu_buf = [area(12288 + 512 * i, 512) for i in range(2)]
        slot_high = [part_area(13312 + SLOT * i, SLOT) for i in range(2)]
        GA = 0

        def ga(cols, pattern=None, **dims):
            nonlocal GA
            GA += cols
            return area(GA - cols, cols, pattern, **dims)

        fT = ga(1024, "p (g t) -> p g t", g=4)
        q_ro = ga(512, "p (c t) -> p c t", c=2)
        k_ro = ga(1024, "p (c t) -> p c t", c=2)
        g_silu = ga(1024, "p (h t) -> p h t", h=4)
        v_gla = ga(2048, "p (t c) -> p t c", t=4)
        lowT = ga(512)
        z_buf = ga(2048, "p (d c t) -> p d c t", d=2, c=2)
        cum = ga(2048, "p (d c t) -> p d c t", d=2, c=2)
        soft = ga(2048, "p (d c t) -> p d c t", d=2, c=2)
        qe = ga(1024, "p (d c t) -> p d c t", d=2, c=2)
        ke = ga(1024, "p (d c t) -> p d c t", d=2, c=2)
        k_dec = soft
        kd_tok = ga(2048, "p (d c t e) -> p d c t e", d=2, c=2, t=4)
        states = ga(2048, "p (d c n e) -> p d c n e", d=2, c=2, n=4)
        running = ga(512, "p (d c e) -> p d c e", d=2, c=2)
        attT = ga(2048, "p (d h t l) -> p d h t l", d=2, h=4, t=2)
        decay = ga(32, "p (d c n) -> p d c n", d=2, c=2)
        oT = ga(1024, "p (h t) -> p h t", h=4)
        o_sq = z_buf.rearrange("p d c t -> p (d c t)")[:, 0:1024].rearrange("p (h t) -> p h t", h=4)
        o_rstd = z_buf.rearrange("p d c t -> p (d c t)")[:, 1024:2048].rearrange("p (h t) -> p h t", h=4)
        dft_ab = cum.rearrange("p d c t -> p (d c t)").rearrange("p (g t e) -> p g t e", g=4, t=2)
        rope_tmp = ga(1024, "p (c t) -> p c t", c=4)
        q_aT = area(0, 1024, "p (c t) -> p c t", c=4)
        cT = area(1024, 256)
        q_iT = area(1280, 1024, "p (c t) -> p c t", c=4)
        k_iT = area(2304, 256)
        q_bT = area(2560, 1024, "p (c t) -> p c t", c=4)
        k_bT = area(3584, 256)
        v_b = area(3840, 256, "p (t e) -> p t e", t=2)
        c_tok = area(4096, 256, "p (t e) -> p t e", t=2)
        q_lat = area(4352, 2048, "p (h t) -> p h t", h=8)
        relu_buf = [area(6400 + 256 * i, 256) for i in range(2)]
        idx_score = area(6912, 512, "p (t k) -> p t k", t=2)
        idx_work = area(7424, 512, "p (t k) -> p t k", t=2)
        o_lat = area(7936, 2048, "p (h t) -> p h t", h=8)
        c_sq = area(9984, 256)
        w_heads = area(10240, 16, "p (t h) -> p t h", t=2)
        top8 = area(10256, 16, "p (t n) -> p t n", t=2)
        q_oT = area(0, 2048, "p (c t) -> p c t", c=8)
        kcT, vcT, ksT, kwT = (area(2048 + 256 * i, 256) for i in range(4))
        vs_vw = area(3072, 512, "p (t e) -> p t e", t=2)
        blk = [area(3584 + 512 * i, 480, "p (q n) -> p q n", q=32) for i in range(2)]
        hid = [area(4608 + 32 * i, 32, "p (g n) -> p g n", g=2) for i in range(2)]
        kcmpT = area(4672, 16)
        v_cmp = area(4704, 128, "p (g e) -> p g e", g=2)
        gates = area(4832, 96, "p (t e) -> p t e", t=2)
        xq = area(0, 1024, "p (c t) -> p c t", c=4)
        xk = area(1024, 1024, "p (c t) -> p c t", c=4)
        xvv = area(2048, 1024, "p (t e) -> p t e", t=2)
        x_tok = area(0, 2048, "p (t e) -> p t e", t=2)
        x_e = area(2048, 1024, "p (c s) -> p c s", c=DC)
        e_low = part_area(3072, 512, "p (f s) -> p f s", f=FB)
        e_high = part_area(3584, 512, "p (f s) -> p f s", f=FB)
        e_silu = [area(4096 + 128 * i, 128) for i in range(2)]
        e_acc = area(4352, 1024)
        pick = area(5376, 256, "p (t s) -> p t s", t=2)
        pick_g = area(5632, 256, "p (t s) -> p t s", t=2)
        pick_gT = area(5888, 256)
        moe_acc = area(6144, 2048, "p (c t) -> p c t", c=DC)
        MO = 8192
        logits = area(MO, 16, "p (t e) -> p t e", t=2)
        top_l = area(MO + 16, 16, "p (t e) -> p t e", t=2)
        top_i = area(MO + 32, 16, "p (t e) -> p t e", t=2)
        WIDTH = 2 * (EXPERTS * PASSES + 1)
        e_gate, e_in, e_pos = (area(MO + 48 + WIDTH * n, WIDTH, "p (t e) -> p t e", t=2) for n in range(3))
        e_tmp = area(MO + 150, 32, "p (t e) -> p t e", t=2)
        e_one = area(MO + 182, 16, "p (t e) -> p t e", t=2)
        passes_f = area(MO + 198, 8)
        block = ctx.enter_context(nc.Block())

        def expert_times(eng):
            return eng.value_load(whole[0:1, 0:1], min_val=EXPERTS, max_val=EXPERTS * PASSES)

        def full(b):
            return sem(f"bank_full{b}")

        def free(b):
            return sem(f"bank_free{b}")

        class Book(Tally):

            def __init__(self, eng):
                super().__init__()
                self.eng, self.turn, self.turns_per, self.t_i = eng, 0, 0, None
                self.extra = 0

            def _uses(self, turn):
                k = turn // BANKS + self.extra
                return k if self.t_i is None else k + self.t_i * (self.turns_per // BANKS)

            def next_bank(self):
                self.turn += 1
                return (self.turn - 1) % BANKS

            def emptied(self):
                return self._uses(self.turn - 1)

            def filled(self):
                return self._uses(self.turn - 1) + 1

            def freed(self, turn):
                return free(turn % BANKS), self._uses(turn) + 1

            def all_freed(self, first, n):
                return [self.freed(t) for t in range(max(first, first + n - BANKS), first + n)]

            def enter(self, i, turns, per):
                assert turns % BANKS == 0
                super().enter(i, per)
                self.t_i, self.turns_per, self.t0 = i, turns, self.turn

            def leave(self, times):
                assert self.turn - self.t0 == self.turns_per, self.turn - self.t0
                self.t_i = None
                if not isinstance(times, int):
                    self.extra = (times - 1) * (self.turns_per // BANKS)
                    super().leave(1)
                    return
                self.turn = self.t0 + self.turns_per * times
                super().leave(times)

        class Weights:

            def __init__(self, book):
                self.book, self.t, self.i, self.per = book, 0, None, 0

            def landed(self):
                n = self.t // TILES
                v = 16 * (n // RING + 1)
                if self.i is not None:
                    v = v + self.i * (16 * self.per // RING)
                self.book.eng.wait_ge(sem(f"slot_landed{n % RING}"), v)

            def tiles(self, n=1):
                first = self.t % TILES == 0
                if first:
                    self.landed()
                at = self.t // TILES % RING * SLOT + self.t % TILES * P
                self.t += n
                return ring[:, at:at + n * P], first

            def slots(self, n):
                at = []
                for _ in range(n):
                    self.landed()
                    at.append(self.t // TILES % RING * SLOT)
                    self.t += TILES
                return [ring[:, a:a + SLOT] for a in at]

            def enter(self, i, slots):
                assert slots % RING == 0 and self.t % TILES == 0
                self.i, self.per, self.t0 = i, slots, self.t

            def leave(self, times):
                assert self.t - self.t0 == self.per * TILES
                self.t = self.t0 + self.per * TILES * times
                self.i = None

        def products(book, w, n_out, rhs, cols, kc=DC, ready=None):
            for n in range(n_out):
                b = book.next_bank()
                book.eng.wait_ge(free(b), book.emptied())
                for k in range(kc):
                    if n == 0 and ready:
                        ready(k)
                    tile, first = w.tiles()
                    m = nc.tensor.matmul(PS[b][:, 0:cols], tile, rhs(k), start=k == 0, stop=k == kc - 1)
                    if first:
                        m.then_inc(sem("slots_used"), 1)
                m.then_inc(full(b), 1)

        def token_products(book, w, lhs, tiles, n=2, cols=512):
            parts = w.slots(n)
            per = SLOT // cols
            for t in range(tiles):
                b = book.next_bank()
                book.eng.wait_ge(free(b), book.emptied())
                for k in range(DC):
                    s, j = k // per, k % per
                    m = nc.tensor.matmul(PS[b][:, 0:cols], lhs(k, t), parts[s][:, j * cols:(j + 1) * cols],
                                         start=k == 0, stop=k == DC - 1)
                    if j == 0 and ((s == 0 and t == 0) or (s > 0 and t == tiles - 1)):
                        m.then_inc(sem("slots_used"), 1)
                m.then_inc(full(b), 1)

        def sum_pe(book, name, at, cols, chunks=DC):
            b = book.next_bank()
            book.eng.wait_ge(free(b), book.emptied())
            for c in range(chunks):
                if name:
                    book.eng.wait_ge(sem(name), book.up(name))
                m = nc.tensor.matmul(PS[b][:, 0:cols], ones, at(c), start=c == 0, stop=c == chunks - 1)
            m.then_inc(full(b), 1)

        def root_act(book, cols, eps_at, n=D, to=None):
            b = book.next_bank()
            book.eng.wait_ge(full(b), book.filled())
            to = rstd[:, 0:cols] if to is None else to
            nc.scalar.activation(to, PS[b][:, 0:cols], ACT.Sqrt, bias=small_at("eps")[:, eps_at:eps_at + 1],
                                 scale=1.0 / n).then_inc(free(b), 1)

        def root_dve(book, cols, to=None):
            to = rstd[:, 0:cols] if to is None else to
            book.turn += 1
            book.eng.wait_ge(*book.freed(book.turn - 1))
            nc.vector.reciprocal(to, to).then_inc(sem("dve_step"), 1)
            book.eng.wait_ge(sem("dve_step"), book.up("dve_step"))

        def squares_act(book, cols, ready):
            for c in range(DC):
                ready(c)
                nc.scalar.activation(sqv[:, c, 0:cols], xv[:, c, 0:cols], ACT.Square).then_inc(sem("squared"), 1)

        def rms_act(book, l, m, sides, ready):
            squares_act(book, SEQ * sides, ready)
            root_act(book, SEQ * sides, 0)
            for c in range(DC):
                for s in range(sides):
                    t = slice(SEQ * s, SEQ * (s + 1))
                    book.eng.wait_ge(sem("scaled"), book.up("scaled"))
                    nc.scalar.activation(hv[:, c, t], hv[:, c, t], ACT.Identity, bias=shift(l, m, c, s))\
                        .then_inc(sem("h_ready"), 1)

        def rms_dve(book, l, m, sides):
            root_dve(book, SEQ * sides)
            for c in range(DC):
                for s in range(sides):
                    t = slice(SEQ * s, SEQ * (s + 1))
                    nc.vector.scalar_tensor_tensor(hv[:, c, t], xv[:, c, t], scalev[:, l, m, c, s:s + 1],
                                                   rstd[:, t], ALU.mult, ALU.mult).then_inc(sem("scaled"), 1)

        def residual_dve(book, l, m, sides, between=None):
            for c in range(DC):
                b = book.next_bank()
                book.eng.wait_ge(full(b), book.filled())
                for s in range(sides):
                    t = slice(SEQ * s, SEQ * (s + 1))
                    last = nc.vector.scalar_tensor_tensor(xv[:, c, t], PS[b][:, t], gain(l, m, c, s), xv[:, c, t],
                                                          ALU.mult, ALU.add)
                last.then_inc(free(b), 1)
                if between:
                    between(c)

        X2 = slice(0, SEQ)

        def ln_pe(book, ready):
            b = book.next_bank()
            book.eng.wait_ge(free(b), book.emptied())
            for c in range(DC):
                ready(c)
                m = nc.tensor.matmul(PS[b][:, X2], ones, xv[:, c, X2], start=c == 0, stop=c == DC - 1)
            m.then_inc(full(b), 1)
            sum_pe(book, "squared", lambda c: sqv[:, c, X2], SEQ)

        def ln_act(book, n):
            b = book.next_bank()
            book.eng.wait_ge(full(b), book.filled())
            nc.scalar.activation(mean[:, :], PS[b][:, X2], ACT.Identity, scale=1.0 / D).then_inc(free(b), 1)
            for c in range(DC):
                book.eng.wait_ge(sem("centred"), book.up("centred"))
                nc.scalar.activation(sqv[:, c, X2], xv[:, c, X2], ACT.Square).then_inc(sem("squared"), 1)
            root_act(book, SEQ, 1)
            for c in range(DC):
                book.eng.wait_ge(sem("scaled"), book.up("scaled"))
                nc.scalar.activation(xv[:, c, X2], xv[:, c, X2], ACT.Identity,
                                     bias=small_at("ln_b")[:, n * DC + c:n * DC + c + 1]).then_inc(sem("ln_ready"), 1)

        def ln_dve(book, n):
            book.turn += 1
            book.eng.wait_ge(*book.freed(book.turn - 1))
            for c in range(DC):
                nc.vector.tensor_tensor(xv[:, c, X2], xv[:, c, X2], mean[:, :], ALU.subtract)\
                    .then_inc(sem("centred"), 1)
            book.up("centred", DC)
            root_dve(book, SEQ)
            for c in range(DC):
                nc.vector.scalar_tensor_tensor(xv[:, c, X2], xv[:, c, X2],
                                               small_at("ln_g")[:, n * DC + c:n * DC + c + 1], rstd[:, X2],
                                               ALU.mult, ALU.mult).then_inc(sem("scaled"), 1)

        def ln_residual_dve(book, between=None):
            for c in range(DC):
                b = book.next_bank()
                book.eng.wait_ge(full(b), book.filled())
                nc.vector.scalar_tensor_tensor(xv[:, c, X2], xv[:, c, X2], ALPHA, PS[b][:, X2], ALU.mult, ALU.add)\
                    .then_inc(free(b), 1)
                if between:
                    between(c)

        def round_dve(book, high, value):
            nc.vector.tensor_copy(high, value).then_inc(sem("rounded"), 1)
            book.eng.wait_ge(sem("rounded"), book.up("rounded"))

        def low_dve(low, value, high):
            return nc.vector.tensor_tensor(low, value, high.bitcast(F32), ALU.subtract)

        def split_slot(book, n, i, used=None, per=RING):
            if used is not None:
                book.eng.wait_ge(sem("slots_used"), used if i is None else used + i * per)
            landed = 16 * (n // RING + 1)
            book.eng.wait_ge(sem(f"slot_landed{n % RING}"), landed if i is None else landed + i * (16 * per // RING))
            at, high = slice(n % RING * SLOT, (n % RING + 1) * SLOT), slot_high[n % 2]
            round_dve(book, high, ring[:, at])
            low_dve(ring_part[:, at], ring[:, at], high).then_inc(sem("slot_split"), 1)

        def split_input(book, ready, per, src, cols):
            for c in range(DC):
                book.eng.wait_ge(sem(ready), book.up(ready, per))
                round_dve(book, in_high[:, c, 0:cols], src[:, c, 0:cols])
                low_dve(h_part[:, c, 0:cols], src[:, c, 0:cols], in_high[:, c, 0:cols])\
                    .then_inc(sem("in_split"), 1)

        def split_product(book, w, out_ap, high, low, start, stop):
            first = w.t % TILES == 0
            if first:
                book.eng.wait_ge(sem("slot_split"), book.up("slot_split"))
            n, at = w.t // TILES, w.t % TILES * P
            w.t += 1
            w_high = slot_high[n % 2][:, at:at + P]
            w_low = ring_part[:, n % RING * SLOT + at:n % RING * SLOT + at + P]
            m = nc.tensor.matmul(out_ap, w_high, high, start=start, stop=False)
            if first:
                m.then_inc(sem("slots_used"), 1)
            nc.tensor.matmul(out_ap, w_high, low, start=False, stop=False)
            return nc.tensor.matmul(out_ap, w_low, high, start=False, stop=stop)

        def ffn_block_pe(book, w, low, cols, nf, first_use=False):
            for n in range(2 * nf):
                b = book.next_bank()
                book.eng.wait_ge(free(b), book.emptied())
                for k in range(DC):
                    if first_use and n == 0:
                        book.eng.wait_ge(sem("in_split"), book.up("in_split"))
                    m = split_product(book, w, PS[b][:, 0:cols], in_high[:, k, 0:cols], low[:, k, 0:cols],
                                      k == 0, k == DC - 1)
                m.then_inc(full(b), 1)
            for n in range(DC):
                b = book.next_bank()
                book.eng.wait_ge(free(b), book.emptied())
                for k in range(nf):
                    if n == 0:
                        book.eng.wait_ge(sem("act_split"), book.up("act_split"))
                    m = split_product(book, w, PS[b][:, 0:cols], act_high[:, k, 0:cols], act_low[:, k, 0:cols],
                                      k == 0, k == nf - 1)
                m.then_inc(full(b), 1)

        def ffn_block_act(book, cols, nf):
            for f in range(nf):
                back = book.turn - 3 if f >= 2 else book.turn - 3 - DC
                book.eng.wait_ge(*book.freed(back))
                b = book.next_bank()
                book.eng.wait_ge(full(b), book.filled())
                nc.scalar.activation(silu_buf[f % 2][:, 0:cols], PS[b][:, 0:cols], ACT.Silu).then_inc(free(b), 1)
                book.turn += 1
            book.turn += DC

        def ffn_block_dve(book, cols, nf, n, i, ahead):
            todo = list(range(n + 2, n + ahead))
            for f in range(nf):
                book.eng.wait_ge(*book.freed(book.turn))
                book.turn += 1
                b = book.next_bank()
                book.eng.wait_ge(full(b), book.filled())
                low, high = act_low[:, f, 0:cols], act_high[:, f, 0:cols]
                nc.vector.tensor_tensor(act_buf[:, 0:cols], silu_buf[f % 2][:, 0:cols], PS[b][:, 0:cols], ALU.mult)\
                    .then_inc(free(b), 1)
                book.eng.wait_ge(*book.freed(book.turn - 1))
                round_dve(book, high, act_buf[:, 0:cols])
                low_dve(low, act_buf[:, 0:cols], high).then_inc(sem("act_split"), 1)
                if todo:
                    split_slot(book, todo[0], i, used=todo.pop(0))
            for c in range(DC):
                b = book.next_bank()
                book.eng.wait_ge(full(b), book.filled())
                if c == 0:
                    book.eng.wait_ge(*book.freed(book.turn - 2 * nf - 2))
                nc.vector.tensor_tensor(down_acc[:, c, 0:cols], down_acc[:, c, 0:cols], PS[b][:, 0:cols],
                                        ALU.add).then_inc(free(b), 1)
                if todo and c % 4 == 3:
                    split_slot(book, todo[0], i, used=todo.pop(0))

        FFN_LOOPS, FFN_REST = FC // FB, FC % FB
        SLOTS_BLOCK = FB * 3 * DC // TILES
        assert SLOTS_BLOCK == RING

        def ffn_pe(book, w, low, cols):
            assert w.t in [at * TILES for at in FFN_AT]
            ffn_block_pe(book, w, low, cols, FB, first_use=True)
            with nc.tensor.Fori(0, FFN_LOOPS - 1) as i:
                book.enter(i, 16, {"act_split": FB, "slot_split": SLOTS_BLOCK})
                w.enter(i, SLOTS_BLOCK)
                ffn_block_pe(book, w, low, cols, FB)
                book.leave(FFN_LOOPS - 1)
                w.leave(FFN_LOOPS - 1)
            ffn_block_pe(book, w, low, cols, FFN_REST)

        def ffn_act(book, cols):
            with nc.scalar.Fori(0, FFN_LOOPS) as i:
                book.enter(i, 16, {})
                ffn_block_act(book, cols, FB)
                book.leave(FFN_LOOPS)
            ffn_block_act(book, cols, FFN_REST)

        def ffn_begin_dve(book, j, cols):
            def between(c):
                if c == 1:
                    split_slot(book, FFN_AT[j], None)
                elif c == 4:
                    split_slot(book, FFN_AT[j] + 1, None)
                elif c == 2:
                    nc.vector.memset(down_acc[:, :, 0:cols], 0.0)
            return between

        def ffn_dve(book, j, cols):
            with nc.vector.Fori(0, FFN_LOOPS) as i:
                book.enter(i, 16, {"rounded": FB + SLOTS_BLOCK})
                ffn_block_dve(book, cols, FB, FFN_AT[j], i, SLOTS_BLOCK + 2)
                book.leave(FFN_LOOPS)
            ffn_block_dve(book, cols, FFN_REST, FFN_AT[j] + FFN_LOOPS * SLOTS_BLOCK, None, FFN_REST * 3 * DC // TILES)
            book.eng.wait_ge(*book.freed(book.turn - 1))

        def order(n):
            for a in range(n + 3):
                if a < n:
                    yield "S", a
                if 0 <= a - 2 < n:
                    yield "T", a - 2
                if 0 <= a - 3 < n:
                    yield "V", a - 3

        def attention_pe(book, jobs):
            turn_of = {}
            for what, a in order(len(jobs)):
                j = jobs[a]
                nk = j["nk"]
                b = book.next_bank()
                book.eng.wait_ge(free(b), book.emptied())
                turn_of[what, a] = book.turn - 1
                if what == "S":
                    m = nc.tensor.matmul(PS[b][:, 0:nk], j["q"], j["k"], start=True, stop=True)
                elif what == "T":
                    book.eng.wait_ge(sem("probs_ready"), book.up("probs_ready"))
                    e = exp_buf[a % 3]
                    for t in range(0, nk, P):
                        n = min(P, nk - t)
                        m = nc.tensor.transpose(PS[b][0:n, t:t + P], e[:, t:t + n], ident)
                else:
                    book.eng.wait_ge(*book.freed(turn_of["T", a]))
                    o, n_v = j["out"], len(j["v"])
                    p0 = j["p0"]
                    for i, v in enumerate(j["v"]):
                        kk = v.shape[0]
                        m = nc.tensor.matmul(PS[b][p0:p0 + o.shape[0], 0:P], v,
                                             pt_buf[a % 2][0:kk, i * P:(i + 1) * P],
                                             start=i == 0, stop=i == n_v - 1)
                m.then_inc(full(b), 1)

        def attention_act(book, jobs):
            for what, a in order(len(jobs)):
                j = jobs[a]
                nk = j["nk"]
                if what == "S":
                    book.turn += 1
                    book.eng.wait_ge(sem("scores_ready"), book.up("scores_ready"))
                    w = nk + (j["sink"] is not None)
                    nc.scalar.activation(exp_buf[a % 3][:, 0:w], score_buf[a % 3][:, 0:w], ACT.Exp,
                                         bias=stats[:, a % 4:a % 4 + 1], accum_out=stats[:, 4 + a % 4:5 + a % 4])\
                        .then_inc(sem("exp_ready"), 1)
                elif what == "T":
                    b = book.next_bank()
                    book.eng.wait_ge(full(b), book.filled())
                    rows = min(P, nk)
                    cols = -(-nk // P) * P
                    nc.scalar.activation(pt_buf[a % 2][0:rows, 0:cols], PS[b][0:rows, 0:cols], ACT.Copy)\
                        .then_inc(free(b), 1)
                else:
                    b = book.next_bank()
                    book.eng.wait_ge(full(b), book.filled())
                    if not j["add"]:
                        o, p0 = j["out"], j["p0"]
                        nc.scalar.activation(o, PS[b][p0:p0 + o.shape[0], 0:P], ACT.Copy).then_inc(free(b), 1)

        def attention_dve(book, jobs):
            def scale(a):
                j = jobs[a]
                r = stats[:, 8 + a % 4:9 + a % 4]
                book.eng.wait_ge(sem("exp_ready"), book.up("exp_ready"))
                nc.vector.reciprocal(r, stats[:, 4 + a % 4:5 + a % 4]).then_inc(sem("dve_step"), 1)
                book.eng.wait_ge(sem("dve_step"), book.up("dve_step"))
                if j["gate"] is not None:
                    nc.vector.tensor_tensor(r, r, j["gate"], ALU.mult).then_inc(sem("dve_step"), 1)
                    book.eng.wait_ge(sem("dve_step"), book.up("dve_step"))
                e = exp_buf[a % 3][:, 0:j["nk"]]
                nc.vector.tensor_scalar(e, e, r, None, ALU.mult).then_inc(sem("probs_ready"), 1)

            last_v = None
            for what, a in order(len(jobs)):
                j = jobs[a]
                nk, s = j["nk"], score_buf[a % 3]
                if what == "S":
                    b = book.next_bank()
                    book.eng.wait_ge(full(b), book.filled())
                    w = nk
                    biased = 0 if j["bias"] is None else j["bias"].shape[1]
                    if biased:
                        m = nc.vector.scalar_tensor_tensor(s[:, 0:biased], PS[b][:, 0:biased], j["scale"], j["bias"],
                                                           ALU.mult, ALU.add)
                    if biased < nk:
                        m = nc.vector.tensor_scalar(s[:, biased:nk], PS[b][:, biased:nk], j["scale"], None, ALU.mult)
                    m.then_inc(free(b), 1)
                    book.eng.wait_ge(*book.freed(book.turn - 1))
                    if j["sink"] is not None:
                        w = nk + 1
                        nc.vector.tensor_copy(s[:, nk:nk + 1], j["sink"]).then_inc(sem("dve_step"), 1)
                        book.eng.wait_ge(sem("dve_step"), book.up("dve_step"))
                    if j["mask"] is not None:
                        nc.vector.tensor_tensor(s[:, 0:nk], s[:, 0:nk], j["mask"], ALU.add).then_inc(sem("dve_step"), 1)
                        book.eng.wait_ge(sem("dve_step"), book.up("dve_step"))
                    nc.vector.tensor_reduce(stats[:, a % 4:a % 4 + 1], s[:, 0:w], AX_X, ALU.max, negate=True)\
                        .then_inc(sem("scores_ready"), 1)
                    if a >= 1:
                        scale(a - 1)
                    if a == len(jobs) - 1:
                        scale(a)
                elif what == "T":
                    book.turn += 1
                elif j["add"]:
                    b = book.next_bank()
                    book.eng.wait_ge(full(b), book.filled())
                    book.eng.wait_ge(*book.freed(last_v))
                    o, p0 = j["out"], j["p0"]
                    nc.vector.tensor_tensor(o, o, PS[b][p0:p0 + o.shape[0], 0:P], ALU.add).then_inc(free(b), 1)
                else:
                    book.turn += 1
                if what == "V":
                    last_v = book.turn - 1

        def job(q, k, nk, scale, v, out, p0=0, bias=None, mask=None, sink=None, gate=None, add=False):
            return dict(q=q, k=k, nk=nk, scale=scale, v=v, out=out, p0=p0, bias=bias, mask=mask, sink=sink,
                        gate=gate, add=add)

        def half(h):
            return slice(64 * h, 64 * h + 64)

        def ab_jobs():
            jobs = []
            for h in range(8):
                c, r = h // 2, half(h % 2)
                for t in range(4):
                    lo = 0 if t < 2 else SEQ
                    jobs.append(job(
                        qT[r, c, t * P:(t + 1) * P], kT[r, c, lo:TT], TT - lo, 64 ** -0.5,
                        [v_att[:, n, h * 64:(h + 1) * 64] for n in range(lo // P, 4)],
                        hv[r, 4 + c, t * P:(t + 1) * P], 64 * (h % 2),
                        bias=ab_biasv[:, h, t, :] if t < 2 else None))
            return jobs

        def t5(v, h, t):
            return v[:, h, P:] if t == 0 else v[:, h, :]

        def dsa_jobs():
            return [job(q_lat[:, h, t * P:(t + 1) * P], cT[:, 0:P * (t + 1)], P * (t + 1), 64 ** -0.5,
                        [c_tok[:, n, :] for n in range(t + 1)], o_lat[:, h, t * P:(t + 1) * P],
                        bias=t5(t5v, h, t), mask=idx_work[:, t, 0:P * (t + 1)])
                    for h in range(8) for t in range(2)]

        def band_jobs():
            jobs = []
            for g in range(2):
                for i in range(4):
                    h, r = 4 * g + i, half(g)
                    for t in range(2):
                        jobs.append(job(
                            q_bT[r, i, t * P:(t + 1) * P], k_bT[r, 0:P * (t + 1)], P * (t + 1), 64 ** -0.5,
                            [v_b[:, n, g * 64:(g + 1) * 64] for n in range(t + 1)],
                            hv[r, 4 + i, t * P:(t + 1) * P], 64 * g, bias=t5(bandv, h, t),
                            sink=small_at("sinks")[:, h:h + 1]))
            return jobs

        def cross_jobs():
            return [job(xq[:, h, t * P:(t + 1) * P], xk[:, h, :], SEQ, 128 ** -0.5,
                        [xvv[:, n, h * P:(h + 1) * P] for n in range(2)], hv[:, h, t * P:(t + 1) * P])
                    for h in range(4) for t in range(2)]

        def nsa_jobs():
            jobs = []
            for g in range(2):
                for i in range(8):
                    h, r = 8 * g + i, half(g)
                    for t in range(2):
                        q, o = q_oT[r, i, t * P:(t + 1) * P], hv[r, i, t * P:(t + 1) * P]

                        def gate(n):
                            return gates[:, t, 3 * h + n:3 * h + n + 1]

                        nk = P * (t + 1)
                        jobs.append(job(q, kwT[r, 0:nk], nk, 64 ** -0.5,
                                        [vs_vw[:, n, P + g * 64:P + (g + 1) * 64] for n in range(t + 1)], o, 64 * g,
                                        bias=t5(t5v, h, t), gate=gate(2)))
                        jobs.append(job(q, ksT[r, 0:nk], nk, 64 ** -0.5,
                                        [vs_vw[:, n, g * 64:(g + 1) * 64] for n in range(t + 1)], o, 64 * g,
                                        bias=t5(t5v, h, t), gate=gate(1), add=True))
                        jobs.append(job(q, kcmpT[r, 0:15], 15, 64 ** -0.5, [v_cmp[0:15, g, :]], o, 64 * g,
                                        bias=cmpv[:, t, h, 0:15], gate=gate(0), add=True))
            return jobs


        marks = {}

        @block.tensor
        def _(pe):
            bk = Book(pe)
            w = Weights(bk)
            h_all = lambda k: hv[:, k, :]
            h_x = lambda k: hv[:, k, 0:SEQ]
            x_x = lambda k: xv[:, k, 0:SEQ]

            def h_ready(sides):
                def ready(k):
                    pe.wait_ge(sem("h_ready"), bk.up("h_ready", sides))
                return ready

            def out_products(mixed, sides, kc=DC):
                for taken in bk.all_freed(bk.turn - BANKS, BANKS):
                    pe.wait_ge(*taken)
                products(bk, w, DC, lambda k: mixed(k), SEQ * sides, kc)

            pe.wait_ge(sem("small_landed"), 16)
            pe.wait_ge(sem("silu_c_ready"), 1)

            def ada_products(first_turns=False):
                for _ in range(6):
                    b = bk.next_bank()
                    if not first_turns:
                        pe.wait_ge(free(b), bk.emptied())
                    for k in range(DC):
                        rows, first = w.tiles(4)
                        m = nc.tensor.matmul(PS[b][0:2, :], silu_c[:, 2 * k:2 * k + 2], rows, start=k == 0,
                                             stop=k == DC - 1)
                        if first:
                            m.then_inc(sem("slots_used"), 1)
                    m.then_inc(full(b), 1)
                for half_n in range(2):
                    b = bk.next_bank()
                    if not first_turns:
                        pe.wait_ge(free(b), bk.emptied())
                    for row in bk.all_freed(bk.turn - 7 + 2 * half_n, 3):
                        pe.wait_ge(*row)
                    for n in range(12):
                        at = (12 * half_n + n) * P
                        columns, rows = PS[b][:, 2 * n:2 * n + 2], ada_rows[0:2, at:at + P]
                        if n == 0:
                            nc.tensor.matmul(columns, rows, ident[0:2, 0:2], start=True, stop=True)
                        else:
                            m = nc.tensor.transpose(columns, rows, ident[0:2, 0:2])
                    m.then_inc(full(b), 1)

            ada_products(first_turns=True)
            with nc.tensor.Fori(0, 3) as i:
                bk.enter(i, 8, {})
                w.enter(i, 12)
                ada_products()
                bk.leave(3)
                w.leave(3)

            sum_pe(bk, "squared", lambda c: sqv[:, c, :], TT)
            products(bk, w, 4, h_all, TT, ready=h_ready(2))
            token_products(bk, w, lambda k, t: hv[:, k, t * P:(t + 1) * P], 4)
            products(bk, w, 8, h_all, TT)
            token_products(bk, w, lambda k, t: hv[:, k, t * P:(t + 1) * P], 4)
            pe.wait_ge(sem("ab_landed"), 32)
            pe.wait_ge(sem("v_normed"), bk.up("v_normed", 4))
            for g in range(4):
                b = bk.next_bank()
                pe.wait_ge(free(b), bk.emptied())
                for t in range(4):
                    m = nc.tensor.matmul(PS[b][:, t * P:(t + 1) * P], v_tok[:, t, g * P:(g + 1) * P], sgu_w[:, g, :],
                                         start=True, stop=True)
                m.then_inc(full(b), 1)
            for taken in bk.all_freed(bk.turn - 16, 12):
                pe.wait_ge(*taken)
            attention_pe(bk, ab_jobs())
            pe.wait_ge(sem("sgu_ready"), bk.up("sgu_ready", 4))
            out_products(h_all, 2)
            sum_pe(bk, "squared", lambda c: sqv[:, c, :], TT)
            bk.up("h_ready", 16)
            ffn_pe(bk, w, h_part, TT)

            sum_pe(bk, "squared", lambda c: sqv[:, c, :], TT)
            products(bk, w, 4, h_x, SEQ, ready=h_ready(2))
            products(bk, w, 2, h_x, SEQ)
            products(bk, w, 2, h_all, TT)
            products(bk, w, 4, h_x, SEQ)
            token_products(bk, w, lambda k, t: hv[:, k, t * P:(t + 1) * P], 4)
            b = bk.next_bank()
            pe.wait_ge(free(b), bk.emptied())
            low = small_at("w_lowrank", "p (c n) -> p c n", c=DC)
            for k in range(DC):
                m = nc.tensor.matmul(PS[b][0:32, :], low[:, k, :], hv[:, k, :], start=k == 0, stop=k == DC - 1)
            m.then_inc(full(b), 1)
            pe.wait_ge(*bk.freed(bk.turn - 1))
            wd = small_at("w_decay", "p (d n) -> p d n", d=2)
            for d in range(2):
                for c in range(2):
                    b = bk.next_bank()
                    pe.wait_ge(free(b), bk.emptied())
                    nc.tensor.matmul(PS[b][:, :], wd[0:32, d, c * P:(c + 1) * P], lowT[0:32, :], start=True,
                                     stop=True).then_inc(full(b), 1)
            for taken in bk.all_freed(bk.turn - 17, 4):
                pe.wait_ge(*taken)
            for c in range(4):
                b = bk.next_bank()
                pe.wait_ge(free(b), bk.emptied())
                src = q_ro[:, c, :] if c < 2 else k_ro[:, c - 2, 0:SEQ]
                nc.tensor.matmul(PS[b][:, X2], small_at("rot"), src, start=True, stop=True).then_inc(full(b), 1)
            for taken in bk.all_freed(marks_f := bk.turn - 25, 4):
                pe.wait_ge(*taken)
            for g in range(4):
                b = bk.next_bank()
                pe.wait_ge(free(b), bk.emptied())
                for t in range(2):
                    m = nc.tensor.matmul(PS[b][:, t * SEQ:(t + 1) * SEQ], fT[:, g, t * P:(t + 1) * P],
                                         small_at("dft_ch"), start=True, stop=True)
                m.then_inc(full(b), 1)
            pe.wait_ge(sem("k_decayed"), bk.up("k_decayed", 4))
            for d in range(2):
                for c in range(2):
                    b = bk.next_bank()
                    pe.wait_ge(free(b), bk.emptied())
                    for t in range(4):
                        m = nc.tensor.transpose(PS[b][:, t * P:(t + 1) * P], k_dec[:, d, c, t * P:(t + 1) * P], ident)
                    m.then_inc(full(b), 1)
            for taken in bk.all_freed(bk.turn - 8, 8):
                pe.wait_ge(*taken)
            dcos = small_at("dft_cos", "p (t k) -> p t k", t=2)
            dsin = small_at("dft_nsin", "p (t k) -> p t k", t=2)
            for g in range(4):
                b = bk.next_bank()
                pe.wait_ge(free(b), bk.emptied())
                for t in range(2):
                    nc.tensor.matmul(PS[b][:, X2], dft_ab[:, g, t, 0:P], dcos[:, t, :], start=t == 0, stop=False)
                    m = nc.tensor.matmul(PS[b][:, X2], dft_ab[:, g, t, P:2 * P], dsin[:, t, :], start=False,
                                         stop=t == 1)
                m.then_inc(full(b), 1)
            for d in range(2):
                for c in range(2):
                    for part in range(2):
                        for par in range(2):
                            b = bk.next_bank()
                            pe.wait_ge(free(b), bk.emptied())
                            rows = half(par)
                            for n in range(2):
                                t = n + (2 if part == 0 else 0)
                                for hh in range(2):
                                    m = nc.tensor.matmul(
                                        PS[b][half(hh), n * P:(n + 1) * P], kd_tok[rows, d, c, t, half(hh)],
                                        v_gla[rows, t, (2 * c + hh) * P:(2 * c + hh + 1) * P], start=True, stop=True)
                            m.then_inc(full(b), 1)
            pe.wait_ge(sem("qk_ready"), bk.up("qk_ready", 4))
            for d in range(2):
                for h in range(4):
                    b = bk.next_bank()
                    pe.wait_ge(free(b), bk.emptied())
                    r, c = half(h % 2), h // 2
                    for t in range(2):
                        m = nc.tensor.matmul(PS[b][:, t * P:(t + 1) * P], ke[r, d, c, t * P:(t + 1) * P],
                                             qe[r, d, c, t * P:(t + 1) * P], start=True, stop=True)
                    m.then_inc(full(b), 1)
            for taken in bk.all_freed(bk.turn - 8, 8):
                pe.wait_ge(*taken)
            for h in range(4):
                b = bk.next_bank()
                pe.wait_ge(free(b), bk.emptied())
                for t in range(2):
                    for d in range(2):
                        m = nc.tensor.matmul(PS[b][:, t * P:(t + 1) * P], v_gla[:, t, h * P:(h + 1) * P],
                                             attT[:, d, h, t, :], start=d == 0, stop=d == 1)
                m.then_inc(full(b), 1)
            for taken in bk.all_freed(bk.turn - 28, 16):
                pe.wait_ge(*taken)
            for h in range(4):
                b = bk.next_bank()
                pe.wait_ge(free(b), bk.emptied())
                r, c = half(h % 2), h // 2
                for n in range(4):
                    for d in range(2):
                        m = nc.tensor.matmul(PS[b][:, n * 64:(n + 1) * 64], states[r, d, c, n, :],
                                             qe[r, d, c, n * 64:(n + 1) * 64], start=d == 0, stop=d == 1)
                m.then_inc(full(b), 1)
            for hp in range(2):
                b = bk.next_bank()
                pe.wait_ge(free(b), bk.emptied())
                for hh in range(2):
                    pe.wait_ge(sem("o_squared"), bk.up("o_squared"))
                    m = nc.tensor.matmul(PS[b][:, hh * SEQ:(hh + 1) * SEQ], ones, o_sq[:, 2 * hp + hh, :], start=True,
                                         stop=True)
                m.then_inc(full(b), 1)
            pe.wait_ge(sem("gla_ready"), bk.up("gla_ready", 4))
            out_products(h_x, 1)
            marks["cd_done"] = bk.turn - 8
            sum_pe(bk, "squared", lambda c: sqv[:, c, X2], SEQ)
            ffn_pe(bk, w, h_part, SEQ)
            sum_pe(bk, "squared", lambda c: sqv[:, c, X2], SEQ)
            bk.up("ffn_added", 2 * DC)
            products(bk, w, 15, x_x, SEQ, ready=lambda k: pe.wait_ge(sem("scaled_x"), bk.up("scaled_x")))
            b = bk.next_bank()
            pe.wait_ge(free(b), bk.emptied())
            tiles = [w.tiles()[0] for _ in range(DC)]
            for t in range(2):
                for k in range(DC):
                    m = nc.tensor.matmul(PS[b][:, t * P:(t + 1) * P], xv[:, k, t * P:(t + 1) * P], tiles[k],
                                         start=k == 0, stop=k == DC - 1)
            m.then_inc(full(b), 1)

            def small_token_products(name, n):
                b = bk.next_bank()
                pe.wait_ge(free(b), bk.emptied())
                sw = small_at(name, "p (c n) -> p c n", c=DC)
                for t in range(2):
                    for k in range(DC):
                        m = nc.tensor.matmul(PS[b][:, t * n:(t + 1) * n], xv[:, k, t * P:(t + 1) * P], sw[:, k, :],
                                             start=k == 0, stop=k == DC - 1)
                m.then_inc(full(b), 1)

            small_token_products("w_idx", 8)
            pe.wait_ge(sem("c_squared"), bk.up("c_squared"))
            b = bk.next_bank()
            pe.wait_ge(free(b), bk.emptied())
            nc.tensor.matmul(PS[b][:, X2], ones, c_sq, start=True, stop=True).then_inc(full(b), 1)
            pe.wait_ge(sem("c_ready"), bk.up("c_ready"))
            b = bk.next_bank()
            pe.wait_ge(free(b), bk.emptied())
            for t in range(2):
                m = nc.tensor.transpose(PS[b][:, t * P:(t + 1) * P], cT[:, t * P:(t + 1) * P], ident)
            m.then_inc(full(b), 1)
            uk = small_at("w_uk", "p (c n) -> p c n", c=4)
            for taken in bk.all_freed(bk.turn - 18, 16):
                pe.wait_ge(*taken)
            for h in range(8):
                b = bk.next_bank()
                pe.wait_ge(free(b), bk.emptied())
                r, c = half(h % 2), h // 2
                nc.tensor.matmul(PS[b][:, X2], uk[r, c, :], q_aT[r, c, :], start=True, stop=True).then_inc(full(b), 1)
            for t in range(2):
                for h in range(8):
                    b = bk.next_bank()
                    pe.wait_ge(free(b), bk.emptied())
                    r, c = half(h % 2), h // 2
                    nc.tensor.matmul(PS[b][:, X2], q_iT[r, c, t * P:(t + 1) * P], k_iT[r, :], start=True, stop=True)\
                        .then_inc(full(b), 1)
            for taken in bk.all_freed(bk.turn - 24, 8):
                pe.wait_ge(*taken)
            pe.wait_ge(sem("bias_landed"), 48)
            attention_pe(bk, dsa_jobs())
            uv = small_at("w_uv", "p (h n) -> p h n", h=8)
            for taken in bk.all_freed(bk.turn - BANKS, BANKS):
                pe.wait_ge(*taken)
            for h in range(8):
                b = bk.next_bank()
                pe.wait_ge(free(b), bk.emptied())
                nc.tensor.matmul(PS[b][half(h % 2), X2], uv[:, h, :], o_lat[:, h, :], start=True, stop=True)\
                    .then_inc(full(b), 1)
            attention_pe(bk, band_jobs())
            out_products(h_x, 1)

            def ln(ready):
                ln_pe(bk, ready)

            def last_products(c):
                pe.wait_ge(*bk.freed(bk.turn - 9 + c))

            def cross(n):
                products(bk, w, 4, x_x, SEQ, ready=lambda k: pe.wait_ge(sem("ln_ready"), bk.up("ln_ready")))
                pe.wait_ge(sem("mem_landed"), 16)
                products(bk, w, 4, lambda k: xv[:, k, SEQ:TT], SEQ)
                token_products(bk, w, lambda k, t: xv[:, k, SEQ + t * P:SEQ + (t + 1) * P], 2)
                for taken in bk.all_freed(bk.turn - 10, 10):
                    pe.wait_ge(*taken)
                attention_pe(bk, cross_jobs())
                out_products(h_x, 1, 4)
                ln(last_products)

            ln(last_products)
            cross(0)
            bk.up("ln_ready", 8)
            ffn_pe(bk, w, h_part, SEQ)
            ln(lambda c: pe.wait_ge(sem("ffn_added"), bk.up("ffn_added")))
            products(bk, w, 12, x_x, SEQ, ready=lambda k: pe.wait_ge(sem("ln_ready"), bk.up("ln_ready")))
            token_products(bk, w, lambda k, t: xv[:, k, t * P:(t + 1) * P], 2, n=1, cols=2 * P)
            small_token_products("w_gates", 48)
            for kv in range(2):
                pe.wait_ge(sem("windows_ready"), bk.up("windows_ready"))
                parts = w.slots(2)
                for g in range(2):
                    b = bk.next_bank()
                    pe.wait_ge(free(b), bk.emptied())
                    for q in range(32):
                        s, jj = q // TILES, q % TILES
                        m = nc.tensor.matmul(PS[b][:, 0:15], parts[s][half(g), jj * P:(jj + 1) * P],
                                             blk[kv][half(g), q, :], start=q == 0, stop=q == 31)
                        if jj == 0 and s == g:
                            m.then_inc(sem("slots_used"), 1)
                    m.then_inc(full(b), 1)
            for taken in bk.all_freed(bk.turn - 4, 4):
                pe.wait_ge(*taken)
            b = bk.next_bank()
            pe.wait_ge(free(b), bk.emptied())
            for g in range(2):
                m = nc.tensor.matmul(PS[b][half(g), 0:15], small_at("w2_k"), hid[0][:, g, 0:15], start=True, stop=True)
            m.then_inc(full(b), 1)
            b = bk.next_bank()
            pe.wait_ge(free(b), bk.emptied())
            for g in range(2):
                m = nc.tensor.matmul(PS[b][0:15, g * 64:(g + 1) * 64], hid[1][:, g, 0:15], small_at("w2_v"),
                                     start=True, stop=True)
            m.then_inc(full(b), 1)
            for taken in bk.all_freed(bk.turn - 8, 8):
                pe.wait_ge(*taken)
            attention_pe(bk, nsa_jobs())
            out_products(h_x, 1)
            ln(last_products)
            cross(3)
            pe.wait_ge(sem("ln_ready"), bk.up("ln_ready", 8))
            small_token_products("w_router", EXPERTS)
            for t in range(2):
                for hc in range(2):
                    b = bk.next_bank()
                    pe.wait_ge(free(b), bk.emptied())
                    for c in range(4):
                        m = nc.tensor.transpose(PS[b][:, c * P:(c + 1) * P], xv[:, 4 * hc + c, t * P:(t + 1) * P],
                                                ident)
                    m.then_inc(full(b), 1)
            pe.wait_ge(sem("chosen"), bk.up("chosen", 2))
            b = bk.next_bank()
            pe.wait_ge(free(b), bk.emptied())
            nc.tensor.matmul(PS[b][:, 0:8], small_at("earlier"), e_one[:, 0, :], start=True, stop=True)
            nc.tensor.matmul(PS[b][:, 8:16], ones, e_one[:, 0, :], start=True, stop=False)
            nc.tensor.matmul(PS[b][:, 8:16], small_at("earlier"), e_one[:, 1, :], start=False, stop=True)
            nc.tensor.matmul(PS[b][:, 16:24], ones, e_one[:, 0, :], start=True, stop=False)
            nc.tensor.matmul(PS[b][:, 16:24], ones, e_one[:, 1, :], start=False, stop=True).then_inc(full(b), 1)
            for taken in bk.all_freed(bk.turn - 5, 4):
                pe.wait_ge(*taken)

            def gather():
                pe.wait_ge(sem("picked"), bk.up("picked"))
                for cc in range(4):
                    b = bk.next_bank()
                    pe.wait_ge(free(b), bk.emptied())
                    for c in range(2):
                        for t in range(2):
                            m = nc.tensor.matmul(PS[b][:, c * P:(c + 1) * P],
                                                 x_tok[:, t, (2 * cc + c) * P:(2 * cc + c + 1) * P], pick[:, t, :],
                                                 start=t == 0, stop=t == 1)
                    m.then_inc(full(b), 1)

            def turn_gates():
                pe.wait_ge(sem("picked"), bk.up("picked"))
                for t in range(2):
                    b = bk.next_bank()
                    pe.wait_ge(free(b), bk.emptied())
                    nc.tensor.transpose(PS[b][:, 0:P], pick_g[:, t, :], ident).then_inc(full(b), 1)

            gather()
            turn_gates()
            for taken in bk.all_freed(bk.turn - 6, 6):
                pe.wait_ge(*taken)
            pe.wait_ge(sem("passes_known"), 1)
            times = expert_times(pe)
            with nc.tensor.Fori(0, times) as i:
                bk.enter(i, MOE_TURNS, {"picked": 2, "act_split": FE // P, "slot_split": FE // P // 2})
                w.enter(i, SLOTS_EXPERT)
                for blk_n in range(FE // P // FB):
                    products(bk, w, 2 * FB, lambda k: x_e[:, k, :], P)
                    banks = []
                    for _ in range(2):
                        banks.append(bk.next_bank())
                        pe.wait_ge(free(banks[-1]), bk.emptied())
                    for k in range(FB):
                        pe.wait_ge(sem("act_split"), bk.up("act_split"))
                        for n in range(2):
                            first = w.t % TILES == 0
                            if first:
                                pe.wait_ge(sem("slot_split"), bk.up("slot_split"))
                            slot, at = w.t // TILES, w.t % TILES * P
                            w.t += 4
                            low_at = slot % RING * SLOT + at
                            w_high, w_low = slot_high[slot % 2][:, at:at + 512], ring_part[:, low_at:low_at + 512]
                            acc = PS[banks[n]][:, :]
                            m = nc.tensor.matmul(acc, e_high[:, k, :], w_high, start=k == 0, stop=False)
                            if first:
                                m.then_inc(sem("slots_used"), 1)
                            nc.tensor.matmul(acc, e_high[:, k, :], w_low, start=False, stop=False)
                            m = nc.tensor.matmul(acc, e_low[:, k, :], w_high, start=False, stop=k == FB - 1)
                            if k == FB - 1:
                                m.then_inc(full(banks[n]), 1)
                gather()
                for taken in bk.all_freed(bk.turn - 6, 2):
                    pe.wait_ge(*taken)
                for cc in range(4):
                    b = bk.next_bank()
                    pe.wait_ge(free(b), bk.emptied())
                    for c in range(2):
                        m = nc.tensor.matmul(PS[b][:, c * SEQ:(c + 1) * SEQ],
                                             e_acc[:, (2 * cc + c) * P:(2 * cc + c + 1) * P], pick_gT[:, :],
                                             start=True, stop=True)
                    m.then_inc(full(b), 1)
                turn_gates()
                for taken in bk.all_freed(bk.turn - 10, 4) + bk.all_freed(bk.turn - 2, 2):
                    pe.wait_ge(*taken)
                bk.leave(times)
            ln(lambda c: pe.wait_ge(sem("ffn_added"), bk.up("ffn_added")))

        @block.scalar
        def _(act):
            bk = Book(act)

            def to(dst, func=ACT.Copy, rows=slice(0, P), cols=TT, scale=1.0):
                b = bk.next_bank()
                act.wait_ge(full(b), bk.filled())
                nc.scalar.activation(dst, PS[b][rows, 0:cols], func, scale=scale).then_inc(free(b), 1)

            act.wait_ge(sem("small_landed"), 16)
            nc.scalar.activation(silu_c[:, :], small_at("c2"), ACT.Silu).then_inc(sem("silu_c_ready"), 1)
            act.wait_ge(sem("x_landed"), 32)
            squares_act(bk, TT, lambda c: None)
            with nc.scalar.Fori(0, 4) as i:
                bk.enter(i, 8, {})
                for n in range(6):
                    to(ada_rows[0:2, n * 512:(n + 1) * 512], rows=slice(0, 2))
                for n in range(2):
                    b = bk.next_bank()
                    act.wait_ge(full(b), bk.filled())
                bk.leave(4)
            root_act(bk, TT, 0)
            act.wait_ge(sem("mod_ready"), 4)

            def rms_shift(l, m, sides):
                for c in range(DC):
                    for s in range(sides):
                        t = slice(SEQ * s, SEQ * (s + 1))
                        act.wait_ge(sem("scaled"), bk.up("scaled"))
                        nc.scalar.activation(hv[:, c, t], hv[:, c, t], ACT.Identity, bias=shift(l, m, c, s))\
                            .then_inc(sem("h_ready"), 1)

            rms_shift(0, 0, 2)
            for g in range(4):
                to(uT[:, g, :], ACT.Gelu_apprx_tanh)
            for t in range(4):
                to(v_tok[:, t, :], ACT.Gelu_apprx_tanh)
            act.wait_ge(*bk.freed(bk.turn - 1))
            for t in range(4):
                nc.scalar.activation(v_junk, v_tok[:, t, :], ACT.Square, accum_out=stats[:, 16 + t:17 + t])\
                    .then_inc(sem("act_step"), 1)
                act.wait_ge(sem("act_step"), bk.up("act_step"))
            nc.scalar.activation(stats[:, 20:24], stats[:, 16:20], ACT.Sqrt, bias=small_at("eps")[:, 0:1],
                                 scale=1.0 / 512).then_inc(sem("v_root"), 1)
            for c in range(4):
                to(qT[:, c, :])
            bk.turn += 4 + 4 + 4
            attention_act(bk, ab_jobs())
            bk.turn += DC
            last = lambda c: act.wait_ge(*bk.freed(bk.turn - DC + c))
            added = lambda c: act.wait_ge(sem("ffn_added"), bk.up("ffn_added"))
            rms_act(bk, 0, 1, 2, last)
            ffn_act(bk, TT)
            rms_act(bk, 1, 0, 2, added)
            for g in range(4):
                to(fT[:, g, :], cols=SEQ)
            for c in range(2):
                to(q_ro[:, c, :], cols=SEQ)
            for c in range(2):
                to(k_ro[:, c, :])
            for h in range(4):
                to(g_silu[:, h, :], ACT.Silu, cols=SEQ)
            bk.turn += 4 + 1 + 4 + 4
            for d in range(2):
                for c in range(2):
                    act.wait_ge(*bk.freed(bk.turn - 8 + 2 * d + c))
                    s = soft[:, d, c, :]
                    nc.scalar.activation(s, z_buf[:, d, c, :], ACT.Abs).then_inc(sem("act_step"), 1)
                    act.wait_ge(sem("act_step"), bk.up("act_step"))
                    nc.scalar.activation(s, s, ACT.Exp, scale=-1.0).then_inc(sem("act_step"), 1)
                    act.wait_ge(sem("act_step"), bk.up("act_step"))
                    nc.scalar.activation(s, s, ACT.Ln, bias=1.0).then_inc(sem("log_ready"), 1)
            for d in range(2):
                for c in range(2):
                    act.wait_ge(sem("cum_ready"), bk.up("cum_ready"))
                    nc.scalar.activation(qe[:, d, c, :], cum[:, d, c, X2], ACT.Exp, scale=1 / 16)\
                        .then_inc(sem("exp_b"), 1)
                    nc.scalar.activation(ke[:, d, c, :], cum[:, d, c, X2], ACT.Exp, scale=-1 / 16)\
                        .then_inc(sem("exp_b"), 1)
                    lastb = cum[:, d, c, 63:TT:64] if d == 0 else cum[:, d, c, 0:TT:64]
                    nc.scalar.activation(decay[:, d, c, :], lastb, ACT.Exp, scale=1 / 16).then_inc(sem("exp_b"), 1)
                    act.wait_ge(sem("to_last"), bk.up("to_last"))
                    nc.scalar.activation(z_buf[:, d, c, :], z_buf[:, d, c, :], ACT.Exp, scale=1 / 16)\
                        .then_inc(sem("exp_b"), 1)
            dft_turn = bk.turn
            act.wait_ge(sem("k_decayed"), 4)
            for g in range(4):
                to(dft_ab[:, g, :, :].rearrange("p t e -> p (t e)"))
            for d in range(2):
                for c in range(2):
                    to(kd_tok[:, d, c, :, :].rearrange("p t e -> p (t e)"))
            for g in range(4):
                to(hv[:, g, X2], cols=SEQ)
            bk.turn += 16 + 8
            for h in range(4):
                to(oT[:, h, :], cols=SEQ)
            bk.turn += 4
            for h in range(4):
                act.wait_ge(*bk.freed(bk.turn - 4 + h))
                nc.scalar.activation(o_sq[:, h, :], oT[:, h, :], ACT.Square).then_inc(sem("o_squared"), 1)
            for hp in range(2):
                root_act(bk, TT, 0, n=P, to=o_rstd[:, 2 * hp:2 * hp + 2, :].rearrange("p h t -> p (h t)"))
            bk.turn += DC
            rms_act(bk, 1, 1, 1, last)
            ffn_act(bk, SEQ)
            squares_act(bk, SEQ, added)
            root_act(bk, SEQ, 0)
            for c in range(4):
                to(q_aT[:, c, :], cols=SEQ)
            bk.turn += 1
            for c in range(4):
                to(q_iT[:, c, :], cols=SEQ)
            bk.turn += 1
            for c in range(4):
                to(q_bT[:, c, :], cols=SEQ)
            bk.turn += 1 + 1 + 1
            act.wait_ge(*bk.freed(bk.turn - 13))
            nc.scalar.activation(c_sq, cT, ACT.Square).then_inc(sem("c_squared"), 1)
            root_act(bk, SEQ, 1, n=P)
            to(c_tok[:, :, :].rearrange("p t e -> p (t e)"), cols=SEQ)
            for h in range(8):
                to(q_lat[:, h, :], cols=SEQ)
            for n in range(16):
                if n >= 2:
                    act.wait_ge(sem("score_added"), n - 1)
                to(relu_buf[n % 2], ACT.Relu, cols=SEQ, scale=64 ** -0.5)
            attention_act(bk, dsa_jobs())
            for h in range(8):
                to(hv[half(h % 2), h // 2, X2], rows=half(h % 2), cols=SEQ)
            attention_act(bk, band_jobs())
            bk.turn += DC
            ln_act(bk, 0)

            def cross(n):
                for c in range(4):
                    to(xq[:, c, :], cols=SEQ)
                bk.turn += 6
                attention_act(bk, cross_jobs())
                bk.turn += DC
                ln_act(bk, n)

            cross(1)
            ffn_act(bk, SEQ)
            ln_act(bk, 2)
            for c in range(8):
                to(q_oT[:, c, :], cols=SEQ)
            bk.turn += 4 + 2
            to(gates[:, :, :].rearrange("p t e -> p (t e)"), ACT.Sigmoid, cols=96)
            for kv in range(2):
                for g in range(2):
                    to(hid[kv][:, g, 0:15], ACT.Gelu_apprx_tanh, cols=15)
            bk.turn += 2
            attention_act(bk, nsa_jobs())
            bk.turn += DC
            ln_act(bk, 3)
            cross(4)
            bk.turn += 1
            for t in range(2):
                for hc in range(2):
                    to(x_tok[:, t, hc * 512:(hc + 1) * 512])
            bk.turn += 1
            act.wait_ge(sem("chosen"), bk.up("chosen", 2))
            nc.scalar.activation(stats[:, 34:36], stats[:, 32:34], ACT.Exp).then_inc(sem("top_exp"), 1)

            def gathered():
                for cc in range(4):
                    to(x_e[:, 2 * cc:2 * cc + 2, :].rearrange("p c s -> p (c s)"), cols=SEQ)

            gathered()
            bk.turn += 2
            act.wait_ge(sem("passes_known"), 1)
            times = expert_times(act)
            with nc.scalar.Fori(0, times) as i:
                bk.enter(i, MOE_TURNS, {})
                for blk_n in range(FE // P // FB):
                    for f in range(FB):
                        act.wait_ge(*bk.freed(bk.turn - 3 - (0 if f >= 2 else 2 if blk_n else 12)))
                        to(e_silu[f % 2], ACT.Silu, cols=P)
                        bk.turn += 1
                    bk.turn += 2
                gathered()
                bk.turn += 6
                bk.leave(times)
            ln_act(bk, 5)

        @block.vector
        def _(dve):
            bk = Book(dve)

            def to(dst, rows=slice(0, P), cols=TT):
                b = bk.next_bank()
                dve.wait_ge(full(b), bk.filled())
                nc.vector.tensor_copy(dst, PS[b][rows, 0:cols]).then_inc(free(b), 1)

            dve.wait_ge(sem("small_landed"), 16)
            ada_b = small_at("ada_b")
            with nc.vector.Fori(0, 4) as i:
                bk.enter(i, 8, {})
                bk.turn += 6
                for n in range(2):
                    b = bk.next_bank()
                    dve.wait_ge(full(b), bk.filled())
                    at = bass.ds(i * 48 + 24 * n, 24)
                    nc.vector.tensor_tensor(mod[:, at], PS[b][:, 0:24], ada_b[:, at], ALU.add).then_inc(free(b), 1)
                bk.leave(4)
            dve.wait_ge(*bk.freed(bk.turn - 1))
            for l in range(2):
                for m in range(2):
                    nw = small_at(("norm_mix_w", "norm_ffn_w")[m], "p (l c s) -> p l c s", l=2, c=DC)
                    nc.vector.scalar_tensor_tensor(scalev[:, l, m, :, :], modv[:, l, 24 * m + 8:24 * m + 16, :], 1.0,
                                                   nw[:, l, :, :], ALU.add, ALU.mult).then_inc(sem("mod_ready"), 1)
            dve.wait_ge(sem("mod_ready"), 4)
            dve.wait_ge(sem("x_landed"), 32)
            rms_dve(bk, 0, 0, 2)
            bk.turn += 4 + 4
            bk.turn += 4
            dve.wait_ge(sem("v_root"), bk.up("v_root"))
            nc.vector.reciprocal(stats[:, 20:24], stats[:, 20:24]).then_inc(sem("dve_step"), 1)
            dve.wait_ge(sem("dve_step"), bk.up("dve_step"))
            for t in range(4):
                nc.vector.tensor_scalar(v_tok[:, t, :], v_tok[:, t, :], stats[:, 20 + t:21 + t], None, ALU.mult)\
                    .then_inc(sem("v_normed"), 1)
            for c in range(4):
                to(kT[:, c, :])
            for t in range(4):
                to(v_att[:, t, :])
            dve.wait_ge(sem("ab_landed"), 32)
            for g in range(4):
                b = bk.next_bank()
                dve.wait_ge(full(b), bk.filled())
                in4 = PS[b][:, :].rearrange("p (t q) -> p t q", t=4)
                nc.vector.scalar_tensor_tensor(
                    gate_tmp.rearrange("p (t q) -> p t q", t=4), in4, small_at("sgu_norm_w")[:, g:g + 1],
                    sgu_b[:, g:g + 1, :].broadcast_to([P, 4, P]), ALU.mult, ALU.add).then_inc(free(b), 1)
                dve.wait_ge(*bk.freed(bk.turn - 1))
                nc.vector.tensor_tensor(hv[:, g, :], gate_tmp, uT[:, g, :], ALU.mult).then_inc(sem("sgu_ready"), 1)
                dve.wait_ge(sem("sgu_ready"), bk.up("sgu_ready"))
            attention_dve(bk, ab_jobs())
            residual_dve(bk, 0, 0, 2, between=ffn_begin_dve(bk, 0, TT))
            rms_dve(bk, 0, 1, 2)
            bk.up("h_ready", 16)
            split_input(bk, "h_ready", 2, hv, TT)

            def ffn_residual(l, sides):
                for c in range(DC):
                    for s in range(sides):
                        t = slice(SEQ * s, SEQ * (s + 1))
                        ins = nc.vector.scalar_tensor_tensor(xv[:, c, t], down_acc[:, c, t], gain(l, 1, c, s),
                                                             xv[:, c, t], ALU.mult, ALU.add)
                    ins.then_inc(sem("ffn_added"), 1)
                dve.wait_ge(sem("ffn_added"), bk.up("ffn_added", DC))

            ffn_dve(bk, 0, TT)
            ffn_residual(0, 2)
            rms_dve(bk, 1, 0, 2)
            bk.turn += 4 + 2 + 2 + 4
            for t in range(4):
                to(v_gla[:, t, :])
            to(lowT[0:32, :], rows=slice(0, 32))
            for d in range(2):
                for c in range(2):
                    b = bk.next_bank()
                    dve.wait_ge(full(b), bk.filled())
                    nc.vector.tensor_scalar(z_buf[:, d, c, :], PS[b][:, :],
                                            small_at("decay_b")[:, 2 * d + c:2 * d + c + 1], None, ALU.add)\
                        .then_inc(free(b), 1)
            for taken in bk.all_freed(bk.turn - 17, 4):
                dve.wait_ge(*taken)
            for c in range(4):
                b = bk.next_bank()
                dve.wait_ge(full(b), bk.filled())
                x = q_ro[:, c, :] if c < 2 else k_ro[:, c - 2, X2]
                nc.vector.tensor_tensor(rope_tmp[:, c, :], PS[b][:, X2], small_at("sin"), ALU.mult)\
                    .then_inc(free(b), 1)
                dve.wait_ge(*bk.freed(bk.turn - 1))
                nc.vector.tensor_tensor(x, x, small_at("cos"), ALU.mult).then_inc(sem("dve_step"), 1)
                dve.wait_ge(sem("dve_step"), bk.up("dve_step"))
                nc.vector.tensor_tensor(x, x, rope_tmp[:, c, :], ALU.add).then_inc(sem("dve_step"), 1)
                dve.wait_ge(sem("dve_step"), bk.up("dve_step"))
            starts = small_at("chunk_start")
            for d in range(2):
                for c in range(2):
                    dve.wait_ge(sem("log_ready"), bk.up("log_ready"))
                    z = z_buf[:, d, c, :]
                    nc.vector.scalar_tensor_tensor(z, z, 0.0, soft[:, d, c, :], ALU.min, ALU.subtract).then_inc(sem("dve_step"), 1)
                    dve.wait_ge(sem("dve_step"), bk.up("dve_step"))
                    step = 1 if d == 0 else -1
                    nc.vector.tensor_tensor_scan(cum[:, d, c, ::step], starts, z[:, ::step], 0.0, ALU.mult, ALU.add).then_inc(sem("cum_ready"), 1)
                    dve.wait_ge(sem("cum_ready"), bk.up("cum_ready"))
                    cc = cum[:, d, c, :].rearrange("p (n t) -> p n t", t=64)
                    lastb = cc[:, :, 63:64] if d == 0 else cc[:, :, 0:1]
                    nc.vector.tensor_tensor(z.rearrange("p (n t) -> p n t", t=64), lastb.broadcast_to([P, 8, 64]), cc,
                                            ALU.subtract).then_inc(sem("to_last"), 1)
            for d in range(2):
                for c in range(2):
                    dve.wait_ge(sem("exp_b"), bk.up("exp_b", 4))
                    nc.vector.tensor_tensor(k_dec[:, d, c, :], k_ro[:, c, :], z_buf[:, d, c, :], ALU.mult)\
                        .then_inc(sem("k_decayed"), 1)
                    nc.vector.scalar_tensor_tensor(qe[:, d, c, :], q_ro[:, c, :], 64 ** -0.5, qe[:, d, c, :],
                                                   ALU.mult, ALU.mult)
                    nc.vector.tensor_tensor(ke[:, d, c, :], k_ro[:, c, X2], ke[:, d, c, :], ALU.mult)\
                        .then_inc(sem("qk_ready"), 1)
            bk.turn += 4 + 4 + 4
            for d in range(2):
                for c in range(2):
                    run = running[:, d, c, :]
                    for part in range(2):
                        turns = [bk.turn, bk.turn + 1]
                        banks = []
                        for _ in range(2):
                            banks.append(bk.next_bank())
                            dve.wait_ge(full(banks[-1]), bk.filled())
                        steps = [0, 1, 2, 3] if d == 0 else [3, 2, 1, 0]
                        n_steps = 4 - part
                        for k, n in enumerate(steps[:n_steps]):
                            kv = PS[banks[n % 2]][:, (n // 2) * P:(n // 2 + 1) * P]
                            dec = decay[:, d, c, n + 4 * (1 - part):n + 4 * (1 - part) + 1]
                            if part == 0 and k == 0:
                                ins = nc.vector.tensor_copy(run, kv)
                            else:
                                old = states[:, d, c, n, :] if part else run
                                new = states[:, d, c, steps[k + 1] if part else steps[0], :]
                                ins = nc.vector.scalar_tensor_tensor(new if part or k == 3 else run, old, dec, kv,
                                                                     ALU.mult, ALU.add)
                            if k >= n_steps - 2:
                                ins.then_inc(free(banks[n % 2]), 1)
                                dve.wait_ge(*bk.freed(turns[n % 2]))
                            else:
                                ins.then_inc(sem("dve_step"), 1)
                                dve.wait_ge(sem("dve_step"), bk.up("dve_step"))
            tri = small_at("tri", "p (d l) -> p d l", d=2)
            for d in range(2):
                for h in range(4):
                    b = bk.next_bank()
                    dve.wait_ge(full(b), bk.filled())
                    nc.vector.tensor_tensor(attT[:, d, h, :, :], PS[b][:, X2].rearrange("p (t l) -> p t l", t=2),
                                            tri[:, d:d + 1, :].broadcast_to([P, 2, P]), ALU.mult)\
                        .then_inc(free(b), 1)
            bk.turn += 4
            for h in range(4):
                dve.wait_ge(*bk.freed(bk.turn - 4))
                b = bk.next_bank()
                dve.wait_ge(full(b), bk.filled())
                nc.vector.tensor_tensor(oT[:, h, :], oT[:, h, :], PS[b][:, X2], ALU.add).then_inc(free(b), 1)
            for hp in range(2):
                r = o_rstd[:, 2 * hp:2 * hp + 2, :].rearrange("p h t -> p (h t)")
                root_dve(bk, TT, to=r)
                for h in (2 * hp, 2 * hp + 1):
                    nc.vector.scalar_tensor_tensor(oT[:, h, :], oT[:, h, :], small_at("head_norm_w")[:, 0:1], o_rstd[:, h, :], ALU.mult, ALU.mult).then_inc(sem("dve_step"), 1)
                    dve.wait_ge(sem("dve_step"), bk.up("dve_step"))
                    nc.vector.tensor_tensor(hv[:, 4 + h, X2], oT[:, h, :], g_silu[:, h, :], ALU.mult)\
                        .then_inc(sem("gla_ready"), 1)
            residual_dve(bk, 1, 0, 1, between=ffn_begin_dve(bk, 1, SEQ))
            rms_dve(bk, 1, 1, 1)
            bk.up("h_ready", 16)
            split_input(bk, "h_ready", 1, hv, SEQ)
            ffn_dve(bk, 1, SEQ)
            ffn_residual(1, 1)
            root_dve(bk, SEQ)
            for c in range(DC):
                nc.vector.scalar_tensor_tensor(xv[:, c, X2], xv[:, c, X2], small_at("final_norm_w")[:, c:c + 1],
                                               rstd[:, X2], ALU.mult, ALU.mult).then_inc(sem("scaled_x"), 1)
            bk.turn += 4
            to(cT, cols=SEQ)
            bk.turn += 4
            to(k_iT, cols=SEQ)
            bk.turn += 4
            to(k_bT, cols=SEQ)
            to(v_b[:, :, :].rearrange("p t e -> p (t e)"), cols=SEQ)
            b = bk.next_bank()
            dve.wait_ge(full(b), bk.filled())
            nc.vector.tensor_scalar(w_heads[:, :, :].rearrange("p t h -> p (t h)"), PS[b][:, 0:16], 8 ** -0.5, None,
                                    ALU.mult).then_inc(free(b), 1)
            root_dve(bk, SEQ)
            nc.vector.scalar_tensor_tensor(cT, cT, small_at("ckv_gain"), rstd[:, X2], ALU.mult, ALU.mult)\
                .then_inc(sem("c_ready"), 1)
            bk.turn += 1 + 8
            for t in range(2):
                for h in range(8):
                    dve.wait_ge(*bk.freed(bk.turn))
                    bk.turn += 1
                    wi, s = w_heads[:, t, h:h + 1], idx_score[:, t, :]
                    rb = relu_buf[h % 2]
                    if h == 0:
                        ins = nc.vector.tensor_scalar(s, rb, wi, None, ALU.mult)
                    else:
                        ins = nc.vector.scalar_tensor_tensor(s, rb, wi, s, ALU.mult, ALU.add)
                    ins.then_inc(sem("score_added"), 1)
                    dve.wait_ge(sem("score_added"), bk.up("score_added"))
            for t in range(2):
                dve.wait_ge(sem("score_masked"), t + 1)
                s, wk = idx_score[:, t, :], idx_work[:, t, :]
                for r in range(8):
                    src = s if r == 0 else wk
                    nc.vector.max(top8[:, t, :], src).then_inc(sem("dve_step"), 1)
                    dve.wait_ge(sem("dve_step"), bk.up("dve_step"))
                    nc.vector.match_replace(wk, top8[:, t, :], src, -3e38).then_inc(sem("dve_step"), 1)
                    dve.wait_ge(sem("dve_step"), bk.up("dve_step"))
                nc.vector.tensor_tensor(wk, wk, s, ALU.is_equal).then_inc(sem("dve_step"), 1)
                dve.wait_ge(sem("dve_step"), bk.up("dve_step"))
                nc.vector.tensor_scalar(wk, wk, NEG, None, ALU.mult).then_inc(sem("dve_step"), 1)
                dve.wait_ge(sem("dve_step"), bk.up("dve_step"))
            dve.wait_ge(sem("bias_landed"), 48)
            attention_dve(bk, dsa_jobs())
            bk.turn += 8
            attention_dve(bk, band_jobs())
            ln_residual_dve(bk)
            ln_dve(bk, 0)

            def cross(n, between=None):
                bk.turn += 4
                for c in range(4):
                    to(xk[:, c, :], cols=SEQ)
                for t in range(2):
                    to(xvv[:, t, :])
                attention_dve(bk, cross_jobs())
                ln_residual_dve(bk, between)
                ln_dve(bk, n)

            cross(1, between=ffn_begin_dve(bk, 2, SEQ))
            bk.up("ln_ready", 8)
            split_input(bk, "ln_ready", 1, xv, SEQ)
            ffn_dve(bk, 2, SEQ)

            def acc_residual(acc):
                for c in range(DC):
                    nc.vector.scalar_tensor_tensor(xv[:, c, X2], xv[:, c, X2], ALPHA, acc[:, c, X2], ALU.mult,
                                                   ALU.add).then_inc(sem("ffn_added"), 1)
                dve.wait_ge(sem("ffn_added"), bk.up("ffn_added", DC))

            acc_residual(down_acc)
            ln_dve(bk, 2)
            bk.turn += 8
            for dst in (kcT, vcT, ksT, kwT):
                to(dst, cols=SEQ)
            for kv, (src, pe_name) in enumerate(((kcT, "pe_k"), (vcT, "pe_v"))):
                dve.wait_ge(*bk.freed(bk.turn - 4 + kv))
                win = bass.AP(src.tensor, src.offset, [list(src.ap[0]), [1, 32], [16, 15]])
                emb = small_at(pe_name).rearrange("p (q z) -> p q z", z=1)
                nc.vector.tensor_tensor(blk[kv], win, emb.broadcast_to([P, 32, 15]), ALU.add)\
                    .then_inc(sem("windows_ready"), 1)
            for t in range(2):
                to(vs_vw[:, t, :], cols=2 * P)
            dve.wait_ge(*bk.freed(bk.turn))
            bk.turn += 1
            for t in range(2):
                g0 = gates[:, t, 0:48:3]
                nc.vector.tensor_scalar(g0, g0, small_at("cmp_row_ok")[:, t:t + 1], None, ALU.mult).then_inc(sem("dve_step"), 1)
                dve.wait_ge(sem("dve_step"), bk.up("dve_step"))
            bk.turn += 4
            b = bk.next_bank()
            dve.wait_ge(full(b), bk.filled())
            nc.vector.tensor_copy(kcmpT[:, 0:15], PS[b][:, 0:15]).then_inc(free(b), 1)
            b = bk.next_bank()
            dve.wait_ge(full(b), bk.filled())
            nc.vector.tensor_copy(v_cmp[0:15, :, :].rearrange("p g e -> p (g e)"), PS[b][0:15, 0:P])\
                .then_inc(free(b), 1)
            attention_dve(bk, nsa_jobs())
            ln_residual_dve(bk)
            ln_dve(bk, 3)
            cross(4)
            to(logits[:, :, :].rearrange("p t e -> p (t e)"), cols=16)
            dve.wait_ge(*bk.freed(bk.turn - 1))
            eid = small_at("expert_id")
            for t in range(2):
                nc.vector.max(top_l[:, t, :], logits[:, t, :]).then_inc(sem("dve_step"), 1)
                dve.wait_ge(sem("dve_step"), bk.up("dve_step"))
                nc.vector.max_index(whole[:, 8 * t:8 * t + 8], top_l[:, t, :], logits[:, t, :]).then_inc(sem("dve_step"), 1)
                dve.wait_ge(sem("dve_step"), bk.up("dve_step"))
                nc.vector.tensor_copy(top_i[:, t, :], whole[:, 8 * t:8 * t + 8]).then_inc(sem("dve_step"), 1)
                dve.wait_ge(sem("dve_step"), bk.up("dve_step"))
                nc.vector.tensor_tensor(stats[:, 32 + t:33 + t], top_l[:, t, 1:2], top_l[:, t, 0:1], ALU.subtract).then_inc(sem("dve_step"), 1)
                dve.wait_ge(sem("dve_step"), bk.up("dve_step"))
                nc.vector.tensor_scalar(e_one[:, t, :], eid, top_i[:, t, 0:1], None, ALU.is_equal).then_inc(sem("dve_step"), 1)
                dve.wait_ge(sem("dve_step"), bk.up("dve_step"))
                nc.vector.scalar_tensor_tensor(e_one[:, t, :], eid, top_i[:, t, 1:2], e_one[:, t, :], ALU.is_equal, ALU.add).then_inc(sem("chosen"), 1)
                dve.wait_ge(sem("chosen"), bk.up("chosen"))
            bk.turn += 4
            b = bk.next_bank()
            dve.wait_ge(full(b), bk.filled())
            for ps in range(PASSES):
                for t in range(2):
                    nc.vector.tensor_scalar(e_pos[:, t, 8 * ps:8 * ps + 8], PS[b][:, 8 * t:8 * t + 8],
                                            -float(P * ps), None, ALU.add)
            nc.vector.tensor_reduce(passes_f[:, 0:1], PS[b][:, 16:24], AX_X, ALU.max).then_inc(free(b), 1)
            dve.wait_ge(*bk.freed(bk.turn - 1))
            nc.vector.tensor_scalar(passes_f[:, 1:2], passes_f[:, 0:1], float(P) + 0.5, float(EXPERTS),
                                    ALU.is_ge, ALU.mult).then_inc(sem("dve_step"), 1)
            dve.wait_ge(sem("dve_step"), bk.up("dve_step"))
            nc.vector.tensor_scalar(whole[:, 0:1], passes_f[:, 1:2], float(EXPERTS), None, ALU.add)\
                .then_inc(sem("passes_known"), 1)
            dve.wait_ge(sem("passes_known"), 1)
            dve.wait_ge(sem("top_exp"), bk.up("top_exp"))
            for t in range(2):
                e, w1, w2 = (stats[:, 34 + 2 * n + t:35 + 2 * n + t] for n in range(3))
                nc.vector.tensor_scalar(w1, e, 1.0, None, ALU.add).then_inc(sem("dve_step"), 1)
                dve.wait_ge(sem("dve_step"), bk.up("dve_step"))
                nc.vector.reciprocal(w1, w1).then_inc(sem("dve_step"), 1)
                dve.wait_ge(sem("dve_step"), bk.up("dve_step"))
                nc.vector.tensor_tensor(w2, e, w1, ALU.mult).then_inc(sem("dve_step"), 1)
                dve.wait_ge(sem("dve_step"), bk.up("dve_step"))
                g = e_gate[:, t, 0:8]
                tmp = e_tmp[:, t, 0:8]
                nc.vector.tensor_scalar(tmp, eid, top_i[:, t, 1:2], w2, ALU.is_equal, ALU.mult).then_inc(sem("dve_step"), 1)
                dve.wait_ge(sem("dve_step"), bk.up("dve_step"))
                nc.vector.tensor_scalar(g, eid, top_i[:, t, 0:1], w1, ALU.is_equal, ALU.mult).then_inc(sem("dve_step"), 1)
                dve.wait_ge(sem("dve_step"), bk.up("dve_step"))
                nc.vector.tensor_tensor(g, g, tmp, ALU.add).then_inc(sem("dve_step"), 1)
                dve.wait_ge(sem("dve_step"), bk.up("dve_step"))
                nc.vector.tensor_copy(e_gate[:, t, 8:16], g).then_inc(sem("dve_step"), 1)
                dve.wait_ge(sem("dve_step"), bk.up("dve_step"))
                for ps in range(PASSES):
                    nc.vector.tensor_copy(e_in[:, t, 8 * ps:8 * ps + 8], e_one[:, t, :]).then_inc(sem("dve_step"), 1)
                    dve.wait_ge(sem("dve_step"), bk.up("dve_step"))
            for table in (e_pos, e_in, e_gate):
                nc.vector.memset(table[:, :, EXPERTS * PASSES:], 0.0)
            nc.vector.memset(moe_acc[:, :, :], 0.0).then_inc(sem("dve_step"), 1)
            dve.wait_ge(sem("dve_step"), bk.up("dve_step"))
            cur = stats[:, 48:54].rearrange("p (t n) -> p t n", t=2)

            def choose(n_th):
                for t in range(2):
                    for n, table in enumerate((e_pos, e_in, e_gate)):
                        ins = nc.vector.tensor_copy(cur[:, t, n:n + 1], table[:, t, n_th])
                ins.then_inc(sem("routed"), 1)
                dve.wait_ge(sem("routed"), bk.up("routed"))
                for t in range(2):
                    ins = nc.vector.tensor_scalar(pick[:, t, :], small_at("slot_id"), cur[:, t, 0:1], cur[:, t, 1:2],
                                                  ALU.is_equal, ALU.mult)
                ins.then_inc(sem("picked"), 1)
                dve.wait_ge(sem("picked"), bk.up("picked"))
                for t in range(2):
                    ins = nc.vector.tensor_scalar(pick_g[:, t, :], pick[:, t, :], cur[:, t, 2:3], None, ALU.mult)
                ins.then_inc(sem("picked"), 1)
                dve.wait_ge(sem("picked"), bk.up("picked"))

            def gates_turned():
                for t in range(2):
                    to(pick_gT[:, t * P:(t + 1) * P], cols=P)

            choose(slice(0, 1))
            bk.turn += 4
            gates_turned()
            times = expert_times(dve)
            with nc.vector.Fori(0, times) as i:
                bk.enter(i, MOE_TURNS, {"routed": 1, "picked": 2, "rounded": FE // P + FE // P // 2})
                choose(bass.ds(i + 1, 1))
                for blk_n in range(FE // P // FB):
                    for f in range(FB):
                        dve.wait_ge(*bk.freed(bk.turn))
                        bk.turn += 1
                        b = bk.next_bank()
                        dve.wait_ge(full(b), bk.filled())
                        hid_e = act_buf[:, f % 2 * P:(f % 2 + 1) * P]
                        nc.vector.tensor_tensor(hid_e, e_silu[f % 2], PS[b][:, 0:P], ALU.mult).then_inc(free(b), 1)
                        dve.wait_ge(*bk.freed(bk.turn - 1))
                        round_dve(bk, e_high[:, f, :], hid_e)
                        low_dve(e_low[:, f, :], hid_e, e_high[:, f, :]).then_inc(sem("act_split"), 1)
                        if f in (1, 2):
                            n = N_SLOTS - SLOTS_MOE + blk_n * SLOTS_BLOCK + FB + f - 1
                            split_slot(bk, n, i, used=n - 4, per=SLOTS_EXPERT)
                    if blk_n:
                        dve.wait_ge(*bk.freed(bk.turn - 9))
                    for n in range(2):
                        b = bk.next_bank()
                        dve.wait_ge(full(b), bk.filled())
                        acc = e_acc[:, n * 512:(n + 1) * 512]
                        if blk_n:
                            ins = nc.vector.tensor_tensor(acc, acc, PS[b][:, :], ALU.add)
                        else:
                            ins = nc.vector.tensor_copy(acc, PS[b][:, :])
                        ins.then_inc(free(b), 1)
                bk.turn += 4
                dve.wait_ge(*bk.freed(bk.turn - MOE_TURNS + 3))
                for cc in range(4):
                    b = bk.next_bank()
                    dve.wait_ge(full(b), bk.filled())
                    acc = moe_acc[:, 2 * cc:2 * cc + 2, :].rearrange("p c t -> p (c t)")
                    nc.vector.tensor_tensor(acc, acc, PS[b][:, :], ALU.add).then_inc(free(b), 1)
                gates_turned()
                bk.leave(times)
            dve.wait_ge(*bk.freed(bk.turn - 3))
            acc_residual(moe_acc)
            ln_dve(bk, 5)

        @block.gpsimd
        def _(pool):
            bk = Book(pool)
            pool.dma_start(consts[:, :], small).then_inc(sem("small_landed"), 16)
            pool.dma_start(xv[:, :, 0:SEQ], x_t.rearrange("p (c t) -> p c t", c=DC)).then_inc(sem("x_landed"), 16)
            pool.dma_start(xv[:, :, SEQ:TT], ctx_t.rearrange("p (c t) -> p c t", c=DC)).then_inc(sem("x_landed"), 16)
            pool.dma_start(area(T5, 4096), ab_bias).then_inc(sem("ab_landed"), 16)
            pool.dma_start(area(T5 + 4096, 1024), sgu).then_inc(sem("ab_landed"), 16)
            for taken in bk.all_freed(marks["cd_done"], 8):
                pool.wait_ge(*taken)
            pool.dma_start(xv[:, :, SEQ:TT], mem_t.rearrange("p (c t) -> p c t", c=DC)).then_inc(sem("mem_landed"), 16)
            pool.dma_start(area(T5, 4096), t5_bias).then_inc(sem("bias_landed"), 16)
            pool.dma_start(area(BAND, 2048), band_bias).then_inc(sem("bias_landed"), 16)
            pool.dma_start(area(CMPB, 512), cmp_bias).then_inc(sem("bias_landed"), 16)
            for t in range(2):
                pool.wait_ge(sem("score_added"), 8 * (t + 1))
                nc.gpsimd.affine_select(out=idx_score[:, t, :], in_=idx_score[:, t, :], compare_op=ALU.is_ge,
                                        fill=NEG, base=t * P, pattern=[[-1, SEQ]], channel_multiplier=1)\
                    .then_inc(sem("score_masked"), 1)

        @block.sync
        def _(sp):
            def load(n, i=None, per=0, at=None):
                v = n - RING + 2
                if i is not None:
                    v = v + i * per
                if n >= RING:
                    sp.wait_ge(sem("slots_used"), v)
                at = n if at is None else at
                sp.dma_start(ring[:, n % RING * SLOT:(n % RING + 1) * SLOT], stream[at, :, :])\
                    .then_inc(sem(f"slot_landed{n % RING}"), 16)

            for n in range(RING):
                load(n)
            before = N_SLOTS - SLOTS_MOE
            groups = before // RING
            with nc.sync.Fori(0, groups - 1) as i:
                for n in range(RING, 2 * RING):
                    load(n, i, RING, at=n + i * RING)
            for n in range(groups * RING, before):
                load(n)
            with nc.sync.Fori(0, SLOTS_EXPERT // RING) as i:
                for n in range(before, before + RING):
                    load(n, i, RING, at=n + i * RING)
            sp.wait_ge(sem("passes_known"), 1)
            times = expert_times(sp)
            with nc.sync.Fori(1, times) as i:
                for n in range(before, before + SLOTS_EXPERT):
                    load(n, i, SLOTS_EXPERT, at=n + (i % EXPERTS) * SLOTS_EXPERT)
            sp.wait_ge(sem("ln_ready"), LN_EVENTS)
            sp.dma_start(out.rearrange("p (c t) -> p c t", c=DC), xv[:, :, 0:SEQ]).then_inc(sem("out_stored"), 16)
            sp.wait_ge(sem("out_stored"), 16)


def _by_column(w):
    k, n = w.shape
    return w.reshape(k // P, P, n // P, P).transpose(2, 0, 1, 3).reshape(-1, P, P)


def _by_row(w):
    k, n = w.shape
    return w.reshape(k // P, P, n // P, P).transpose(0, 2, 1, 3).reshape(-1, P, P)


def _ffn_tiles(gate, up, down, by_row=False):
    g = _by_column(gate).reshape(-1, DC, P, P)
    u = _by_column(up).reshape(-1, DC, P, P)
    d = down.reshape(-1, P, DC, P).transpose(0, 2, 1, 3)
    parts = []
    for f in range(0, g.shape[0], FB):
        e = min(f + FB, g.shape[0])
        for j in range(f, e):
            parts += [g[j], u[j]]
        block = d[f:e] if by_row else d[f:e].transpose(1, 0, 2, 3)
        parts.append(block.reshape(-1, P, P))
    return parts


def _paired(n, apart):
    return np.concatenate([np.arange(64) + 64 * h for i in range(apart) for h in (i, i + apart)])[:n]


def _chunked(v, dims=()):
    v = v.reshape(-1, v.shape[-1] // P, P)
    return v.transpose(2, 0, 1).reshape(P, -1)


def _rows(w):
    return w.reshape(-1, P, w.shape[1]).transpose(1, 0, 2).reshape(P, -1)


def _bucket(dist):
    n = np.maximum(dist, 0)
    nf = np.maximum(n, 1).astype(np.float32)
    big = 16 + (np.log(nf / np.float32(16)) / np.float32(math.log(8)) * np.float32(16)).astype(np.int32)
    return np.where(n < 16, n, np.minimum(big, 31))


def _spread(table, index, ok):
    return np.where(ok[..., None], table[index], np.float32(NEG))


def _constants():
    c = {}
    c["ident"], c["ones"] = np.eye(P), np.ones((P, P))
    rot = np.zeros((P, P))
    for m in range(P):
        if m % 32 < 16:
            rot[m + 16, m] = -1
        else:
            rot[m - 16, m] = 1
    c["rot"] = rot
    p, t = np.arange(P)[:, None], np.arange(SEQ)[None, :]
    inv = (np.float32(10000.0) ** (-np.arange(16, dtype=np.float32) / np.float32(16)))[p % 16]
    pos = np.where(p % 64 < 32, t // 64, t % 64).astype(np.float32)
    ang = (pos * inv).astype(np.float32).astype(np.float64)
    c["cos"], c["sin"] = np.cos(ang), np.sin(ang)
    a = 2 * np.pi * np.outer(np.arange(P), np.arange(P)) / P
    norm = 1 / np.sqrt(P * SEQ)
    c["dft_ch"] = np.concatenate([np.cos(a), np.sin(a)], 1) * norm
    b = 2 * np.pi * np.outer(np.arange(SEQ), np.arange(SEQ)) / SEQ
    c["dft_cos"], c["dft_nsin"] = _rows(np.cos(b)), _rows(-np.sin(b))
    m, l = np.arange(P)[:, None], np.arange(P)[None, :]
    same = m // 64 == l // 64
    c["tri"] = np.concatenate([(m <= l) & same, (m >= l) & same], 1)
    c["chunk_start"] = np.broadcast_to(np.arange(TT) % 64 != 0, (P, TT))
    c["expert_id"] = np.broadcast_to(np.arange(EXPERTS), (P, EXPERTS))
    c["cmp_row_ok"] = np.arange(P)[:, None] + P * np.arange(2)[None, :] >= 31
    c["eps"] = np.broadcast_to(np.array([RMS_EPS, LN_EPS]), (P, 2))
    c["slot_id"] = np.broadcast_to(np.arange(P), (P, P))
    c["earlier"] = m < l
    return c


def _small(i):
    s = _constants()
    s["c2"] = np.stack([i["c"][0].reshape(DC, P).T, i["c_ctx"].reshape(DC, P).T], -1).reshape(P, -1)
    s["ada_b"] = np.repeat(_chunked(i["ada_b"]), 2, axis=1)
    s["norm_mix_w"] = np.repeat(_chunked(i["norm_mix_w"]), 2, axis=1)
    s["norm_ffn_w"] = np.repeat(_chunked(i["norm_ffn_w"]), 2, axis=1)
    s["sgu_norm_w"] = _chunked(i["ab_sgu_norm_w"])
    s["final_norm_w"] = _chunked(i["final_norm_w"])
    s["ln_g"], s["ln_b"] = _chunked(i["ln_g_2"]), _chunked(i["ln_b_2"])
    s["ckv_gain"] = _chunked(i["ev_ckv_gain_2"])
    s["decay_b"] = np.concatenate([_chunked(i["cd_decay_b_fwd"]), _chunked(i["cd_decay_b_bwd"])], 1)
    s["head_norm_w"] = _chunked(i["cd_head_norm_w"])
    s["w_idx"] = _rows(i["ev_w_in_2"][0][:, 1216:1224])
    s["w_router"] = _rows(i["moe_w_router_2"][0])
    s["w_gates"] = _rows(i["od_w_in_2"][0][:, 1792:1840])
    s["w_lowrank"] = _rows(i["cd_w_in"][0][:, 2048:2080])
    wd = np.zeros((P, 2, 256), np.float32)
    wd[0:16, 0], wd[16:32, 1] = i["cd_decay_w_fwd"][0], i["cd_decay_w_bwd"][0]
    s["w_decay"] = wd.reshape(P, -1)
    s["w_uk"] = i["ev_w_uk_2"][0].reshape(4, P, P).transpose(1, 0, 2).reshape(P, -1)
    s["w_uv"] = i["ev_w_uv_2"][0].transpose(1, 0, 2).reshape(P, -1)
    s["w2_k"], s["w2_v"] = i["od_w2_k_2"][0], i["od_w2_v_2"][0]
    s["pe_k"], s["pe_v"] = (np.concatenate([i[n][0].T] * 2) for n in ("od_pe_k_2", "od_pe_v_2"))
    s["sinks"] = np.broadcast_to(i["ev_sinks_2"][0], (P, 8))
    table = np.empty((P, N_SMALL), np.float32)
    for name, (at, w) in COL.items():
        table[:, at:at + w] = s[name]
    return table


def _layout(i):
    tiles = [_by_row(w[:, n:n + 512]) for w in i["ada_w"] for n in range(0, 6 * D, 512)]
    w = i["ab_w_in"][0]
    tiles += [_by_column(w[:, 0:512]), _by_row(w[:, 512:1024]), _by_column(w[:, 1024:2048]), _by_row(w[:, 2048:2560])]
    tiles.append(_by_column(i["ab_w_out"][0]))
    tiles += _ffn_tiles(i["ffn_w_gate"][0], i["ffn_w_up"][0], i["ffn_w_down"][0])
    w = i["cd_w_in"][0]
    tiles += [_by_column(w[:, 0:1024]), _by_column(w[:, 1536:2048]), _by_row(w[:, 1024:1536])]
    tiles.append(_by_column(i["cd_w_out"][0]))
    tiles += _ffn_tiles(i["ffn_w_gate"][1], i["ffn_w_up"][1], i["ffn_w_down"][1])
    w = i["ev_w_in_2"][0]
    q_b = w[:, 1224:1736][:, _paired(512, 4)]
    tiles.append(_by_column(np.concatenate(
        [w[:, 0:1152], w[:, 1152:1216], w[:, 1152:1216], q_b, w[:, 1736:1864]], 1)))
    tiles.append(_by_row(w[:, 1864:1992]))
    w = i["ev_w_out_2"][0]
    tiles.append(_by_column(np.concatenate([w[0:512], w[512:1024][_paired(512, 4)]])))

    def cross(l):
        return [_by_column(i["xa_w_q_2"][l]), _by_column(i["xa_w_k_2"][l]), _by_row(i["xa_w_v_2"][l]),
                _by_column(i["xa_w_o_2"][l])]

    tiles += cross(0)
    tiles += _ffn_tiles(i["ff_w_gate_2"][0], i["ff_w_up_2"][0], i["ff_w_down_2"][0])
    w = i["od_w_in_2"][0]
    tiles.append(_by_column(np.concatenate(
        [w[:, 0:1024][:, _paired(1024, 8)], w[:, 1024:1280], w[:, 1280:1408], w[:, 1536:1664]], 1)))
    tiles.append(_by_row(np.concatenate([w[:, 1408:1536], w[:, 1664:1792]], 1)))
    for n in ("od_w1_k_2", "od_w1_v_2"):
        w1 = i[n][0].reshape(32, 64, P)
        tiles.append(np.concatenate([w1, w1], 1))
    tiles.append(_by_column(i["od_w_out_2"][0][_paired(1024, 8)]))
    tiles += cross(1)
    for e in range(EXPERTS):
        tiles += _ffn_tiles(i["moe_w_gate_2"][0, e], i["moe_w_up_2"][0, e], i["moe_w_down_2"][0, e], True)
    stream = np.empty((N_SLOTS, P, TILES, P), np.float32)
    flat, at = stream.transpose(0, 2, 1, 3), 0
    for part in tiles:
        for j in range(0, part.shape[0], DC):
            n = min(DC, part.shape[0] - j)
            flat[at // TILES, at % TILES:at % TILES + n] = part[j:j + n]
            at += n
    assert at == N_SLOTS * TILES, at

    q, k = np.arange(SEQ)[:, None], np.arange(SEQ)[None, :]
    start = np.clip(q % 64 - 8, 0, 48)
    ok = (k % 64 >= start) & (k % 64 < start + 16)
    rb = i["ab_rel_bias"][0][:, k // 64 - q // 64 + 7, np.clip(k % 64 - q % 64 + 15, 0, 30)]
    ab_bias = np.where(ok, rb, np.float32(NEG)).reshape(8, 2, P, SEQ).transpose(2, 0, 1, 3).reshape(P, -1)
    sgu = np.concatenate([i["ab_sgu_w"][0].transpose(2, 0, 1).reshape(P, -1),
                          np.broadcast_to(i["ab_sgu_b"][0].reshape(1, -1), (P, 512))], 1)
    table = i["rel_table_2"]
    dist = P + np.arange(P)[:, None] - np.arange(SEQ)[None, :]
    t5 = _spread(table, _bucket(dist), dist >= 0).transpose(0, 2, 1).reshape(P, -1)
    band = _spread(table[:, 8:16], _bucket(dist), (dist >= 0) & (dist < 128)).transpose(0, 2, 1).reshape(P, -1)
    dist = np.arange(SEQ)[:, None] - (16 * np.arange(16) + 31)[None, :]
    cmp_bias = _spread(table, _bucket(dist), dist >= 0).reshape(2, P, 16, 16).transpose(1, 0, 3, 2).reshape(P, -1)

    def turned(x):
        return x.T.reshape(DC, P, SEQ).transpose(1, 0, 2).reshape(P, -1)

    arrays = [stream.reshape(N_SLOTS, P, SLOT), _small(i), turned(i["x"][0]), turned(i["ctx"][0]),
              turned(i["mem_2"][0]), ab_bias, sgu, t5, band, cmp_bias]
    return [np.ascontiguousarray(a, dtype=np.float32) for a in arrays]


_NAMES = ["stream", "small", "x_t", "ctx_t", "mem_t", "ab_bias", "sgu", "t5_bias", "band_bias", "cmp_bias"]


def kernel(**inputs):
    import concourse.bacc as bacc
    from concourse.bass_utils import run_bass_kernel_spmd

    arrays = _layout({k: np.asarray(v) for k, v in inputs.items()})
    nc = bacc.Bacc("TRN2", target_bir_lowering=False, num_devices=1)
    given, args = {}, []
    for name, a in zip(_NAMES, arrays):
        given[f"in_{name}"] = a
        args.append(nc.dram_tensor(f"in_{name}", a.shape, F32, kind="ExternalInput").ap())
    out = nc.dram_tensor("out", (P, DC * SEQ), F32, kind="ExternalOutput").ap()
    build(nc, *args, out)
    got = run_bass_kernel_spmd(nc, [given], core_ids=[0]).results[0]["out"]
    return got.reshape(P, DC, SEQ).transpose(2, 1, 0).reshape(1, SEQ, D)
```
